# Optimizing a Trainium2 kernel written in Bass

```python
import jax, jax.numpy as jnp
from jax import lax
import numpy as np

D_MODEL = 1024
BATCH = 1
SEQ = 512
DEPTH = 2
DEC_BATCH = 8
DEC_SEQ = 8
PAST_LEN = 1024
PAGE_SIZE = 128

N_META = 16
N_A = DEPTH // 2
N_B = DEPTH - N_A
RET_HEADS = 4
RET_DK = D_MODEL // RET_HEADS
RET_DV = 2 * D_MODEL // RET_HEADS
RET_IN_WIDTH = 2 * RET_HEADS * RET_DK + 2 * RET_HEADS * RET_DV
RET_CHUNK = 128
ROPE_BASE = 10000.0
FOX_HEADS = 16
FOX_DH = D_MODEL // FOX_HEADS
FOX_SCALE = FOX_DH ** -0.5
Q_BLOCK = 128
D_FF = 4 * D_MODEL
EPS = 1e-6
MASK_VALUE = -1e30

kernel_name = 'yoco_retention_fox_decoder'

def rms_norm(x, g=None):
    xf = x.astype(jnp.float32)
    y = xf * lax.rsqrt(jnp.mean(xf * xf, axis=-1, keepdims=True) + EPS)
    if g is not None:
        y = y * g.astype(jnp.float32)
    return y.astype(x.dtype)

def rotary(x, pos):
    half = x.shape[-1] // 2
    inv_freq = ROPE_BASE ** (-jnp.arange(half, dtype=jnp.float32) / half)
    ang = pos.astype(jnp.float32)[:, None] * inv_freq[None, :]
    cos = jnp.cos(ang)[:, None, :]
    sin = jnp.sin(ang)[:, None, :]
    xf = x.astype(jnp.float32)
    x1, x2 = xf[..., :half], xf[..., half:]
    return jnp.concatenate([x1 * cos - x2 * sin, x2 * cos + x1 * sin], axis=-1).astype(x.dtype)

def retention_log_decay():
    return jnp.log1p(-jnp.exp2(-5.0 - jnp.arange(RET_HEADS, dtype=jnp.float32)))

def retention_chunk(S, q, k, v):
    S = S.astype(jnp.float32)
    qf, kf, vf = q.astype(jnp.float32), k.astype(jnp.float32), v.astype(jnp.float32)
    C = q.shape[1]
    lg = retention_log_decay()
    idx = jnp.arange(C, dtype=jnp.float32)
    diff = idx[:, None] - idx[None, :]
    decay = jnp.where(diff >= 0, jnp.exp(lg[:, None, None] * jnp.maximum(diff, 0.0)), 0.0)
    scores = jnp.einsum('bihd,bjhd->bhij', qf, kf) * decay[None]
    intra = jnp.einsum('bhij,bjhe->bihe', scores, vf)
    q_decay = jnp.exp(lg[None, :] * (idx[:, None] + 1.0))
    cross = jnp.einsum('bihd,bhde->bihe', qf, S) * q_decay[None, :, :, None]
    k_decay = jnp.exp(lg[None, :] * (C - 1.0 - idx[:, None]))
    S_new = jnp.exp(lg * C)[None, :, None, None] * S + jnp.einsum('bjhd,bjhe->bhde', kf * k_decay[None, :, :, None], vf)
    return intra + cross, S_new

def retention_prompt(q, k, v):
    B, T = q.shape[:2]
    nc = T // RET_CHUNK

    def to_chunks(a):
        return jnp.moveaxis(a.reshape(B, nc, RET_CHUNK, *a.shape[2:]), 1, 0)

    def step(S, qkv):
        o, S = retention_chunk(S, *qkv)
        return S, o

    S0 = jnp.zeros((B, RET_HEADS, RET_DK, RET_DV), jnp.float32)
    S, o = lax.scan(step, S0, (to_chunks(q), to_chunks(k), to_chunks(v)))
    return jnp.moveaxis(o, 0, 1).reshape(B, T, RET_HEADS, RET_DV), S

def retention_in(x, pos, g, w_in):
    B, T, _ = x.shape
    p = rms_norm(x, g) @ w_in
    q, k, v, gate = jnp.split(p, [RET_HEADS * RET_DK, 2 * RET_HEADS * RET_DK, 2 * RET_HEADS * RET_DK + RET_HEADS * RET_DV], axis=-1)
    q = rotary(q.reshape(B, T, RET_HEADS, RET_DK), pos)
    k = rotary(k.reshape(B, T, RET_HEADS, RET_DK), pos) * (RET_DK ** -0.5)
    v = v.reshape(B, T, RET_HEADS, RET_DV)
    return q, k, v, gate

def retention_out(o, gate, w_out):
    B, T = o.shape[:2]
    o = rms_norm(o).reshape(B, T, RET_HEADS * RET_DV).astype(gate.dtype)
    return (jax.nn.silu(gate) * o) @ w_out

def fox_shared_kv(h, g_kv, w_kvf, b_f, g_k):
    B, T, _ = h.shape
    p = rms_norm(h, g_kv) @ w_kvf
    k, v, f = jnp.split(p, [D_MODEL, 2 * D_MODEL], axis=-1)
    k = rms_norm(k.reshape(B, T, FOX_HEADS, FOX_DH), g_k)
    v = v.reshape(B, T, FOX_HEADS, FOX_DH)
    logf = jax.nn.log_sigmoid((f + b_f).astype(jnp.float32))
    return k, v, logf

def fox_in(x, g, w_qg, g_q):
    B, T, _ = x.shape
    p = rms_norm(x, g) @ w_qg
    q, gate = jnp.split(p, [D_MODEL], axis=-1)
    q = rms_norm(q.reshape(B, T, FOX_HEADS, FOX_DH), g_q)
    return q, gate

def fox_out(o, gate, w_o):
    B, T = o.shape[:2]
    return (o.reshape(B, T, D_MODEL) * jax.nn.sigmoid(gate)) @ w_o

def fox_prompt_attention(q, k, v, cum, valid):
    B, T = q.shape[:2]
    nb = T // Q_BLOCK
    kpos = jnp.arange(T)
    cum_k = jnp.swapaxes(cum, 1, 2)

    def blocks(a):
        return jnp.moveaxis(a.reshape(B, nb, Q_BLOCK, *a.shape[2:]), 1, 0)

    def one_block(args):
        qi, ci, pi = args
        s = jnp.einsum('bqhd,bkhd->bhqk', qi, k).astype(jnp.float32) * FOX_SCALE
        s = s + jnp.swapaxes(ci, 1, 2)[..., :, None] - cum_k[:, :, None, :]
        mask = (kpos[None, :] <= pi[:, None]) & valid[None, :]
        p = jax.nn.softmax(jnp.where(mask, s, MASK_VALUE), axis=-1)
        return jnp.einsum('bhqk,bkhd->bqhd', p.astype(v.dtype), v)

    o = lax.map(one_block, (blocks(q), blocks(cum), kpos.reshape(nb, Q_BLOCK)))
    return jnp.moveaxis(o, 0, 1).reshape(B, T, FOX_HEADS, FOX_DH)

def fox_sample_attention(q, k_past, v_past, cum_past, k_new, v_new, cum_new):
    DS = q.shape[1]
    P = k_past.shape[1]
    s = jnp.concatenate([jnp.einsum('bqhd,bkhd->bhqk', q, k_past),
                         jnp.einsum('bqhd,bkhd->bhqk', q, k_new)], axis=-1).astype(jnp.float32) * FOX_SCALE
    cum_k = jnp.swapaxes(jnp.concatenate([cum_past, cum_new], axis=1), 1, 2)
    s = s + jnp.swapaxes(cum_new, 1, 2)[..., :, None] - cum_k[:, :, None, :]
    causal = jnp.arange(DS)[None, :] <= jnp.arange(DS)[:, None]
    mask = jnp.concatenate([jnp.ones((DS, P), dtype=bool), causal], axis=1)
    p = jax.nn.softmax(jnp.where(mask, s, MASK_VALUE), axis=-1).astype(v_new.dtype)
    return (jnp.einsum('bhqk,bkhd->bqhd', p[..., :P], v_past)
            + jnp.einsum('bhqk,bkhd->bqhd', p[..., P:], v_new))

def mlp(x, g, w_up, w_down):
    return jnp.square(jax.nn.relu(rms_norm(x, g) @ w_up)) @ w_down

def prompt_forward(x_prompt, meta, g_attn, g_mlp, w_ret_in, w_ret_out, g_kv, w_kvf, b_f, g_k,
                   w_fox_qg, g_q, w_fox_out, w_mlp_up, w_mlp_down):
    B = x_prompt.shape[0]
    pad = RET_CHUNK - N_META
    x = jnp.concatenate([jnp.zeros((B, pad, D_MODEL), x_prompt.dtype),
                         jnp.broadcast_to(meta[None], (B, N_META, D_MODEL)).astype(x_prompt.dtype),
                         x_prompt], axis=1)
    T = x.shape[1]
    pos = jnp.arange(T) - pad
    valid = pos >= 0
    ret_states = []
    for l in range(DEPTH):
        if l < N_A:
            q, k, v, gate = retention_in(x, pos, g_attn[l], w_ret_in[l])
            k = k * valid[None, :, None, None].astype(k.dtype)
            o, S = retention_prompt(q, k, v)
            ret_states.append(S)
            x = x + retention_out(o, gate, w_ret_out[l])
        else:
            if l == N_A:
                k_sh, v_sh, logf = fox_shared_kv(x, g_kv, w_kvf, b_f, g_k)
                logf = jnp.where(valid[None, :, None], logf, 0.0)
                cum = jnp.cumsum(logf, axis=1)
            q, gate = fox_in(x, g_attn[l], w_fox_qg[l - N_A], g_q[l - N_A])
            o = fox_prompt_attention(q, k_sh, v_sh, cum, valid)
            x = x + fox_out(o, gate, w_fox_out[l - N_A])
        x = x + mlp(x, g_mlp[l], w_mlp_up[l], w_mlp_down[l])
    y = x[:, pad + N_META:]
    return y, jnp.stack(ret_states), k_sh[:, pad:], v_sh[:, pad:], logf[:, pad:]

def sample_forward(x, state_ret, cache_k, cache_v, cache_logf, page_table, g_attn, g_mlp, w_ret_in,
                   w_ret_out, g_kv, w_kvf, b_f, g_k, w_fox_qg, g_q, w_fox_out, w_mlp_up, w_mlp_down):
    DB, DS, _ = x.shape
    P = page_table.shape[1] * cache_k.shape[1]
    pos = P + jnp.arange(DS)
    ret_states = []
    for l in range(DEPTH):
        if l < N_A:
            q, k, v, gate = retention_in(x, pos, g_attn[l], w_ret_in[l])
            o, S = retention_chunk(state_ret[l], q, k, v)
            ret_states.append(S)
            x = x + retention_out(o, gate, w_ret_out[l])
        else:
            if l == N_A:
                k_new, v_new, logf_new = fox_shared_kv(x, g_kv, w_kvf, b_f, g_k)
                k_past = cache_k[page_table].reshape(DB, P, FOX_HEADS, FOX_DH)
                v_past = cache_v[page_table].reshape(DB, P, FOX_HEADS, FOX_DH)
                cum_past = jnp.cumsum(cache_logf[page_table].reshape(DB, P, FOX_HEADS).astype(jnp.float32), axis=1)
                cum_new = cum_past[:, -1:] + jnp.cumsum(logf_new, axis=1)
            q, gate = fox_in(x, g_attn[l], w_fox_qg[l - N_A], g_q[l - N_A])
            o = fox_sample_attention(q, k_past, v_past, cum_past, k_new, v_new, cum_new)
            x = x + fox_out(o, gate, w_fox_out[l - N_A])
        x = x + mlp(x, g_mlp[l], w_mlp_up[l], w_mlp_down[l])
    return x, jnp.stack(ret_states), k_new, v_new, logf_new

def setup_inputs(seed: int = 0) -> dict:
    key = jax.random.key(seed)
    ks = jax.random.split(key, 24)
    f32 = jnp.float32
    n_pages = PAST_LEN // PAGE_SIZE
    n_used = DEC_BATCH * n_pages
    n_pool = n_used + n_used // 4

    def nrm(k, shape, scale=1.0):
        return jax.random.normal(k, shape, f32) * scale

    return {
        'x_prompt': nrm(ks[0], (BATCH, SEQ, D_MODEL)),
        'x_sample': nrm(ks[1], (DEC_BATCH, DEC_SEQ, D_MODEL)),
        'state_ret': nrm(ks[2], (N_A, DEC_BATCH, RET_HEADS, RET_DK, RET_DV), 0.5),
        'cache_k': nrm(ks[3], (n_pool, PAGE_SIZE, FOX_HEADS, FOX_DH)),
        'cache_v': nrm(ks[4], (n_pool, PAGE_SIZE, FOX_HEADS, FOX_DH)),
        'cache_logf': jax.nn.log_sigmoid(4.0 + nrm(ks[5], (n_pool, PAGE_SIZE, FOX_HEADS))),
        'page_table': jax.random.permutation(ks[6], n_pool)[:n_used].reshape(DEC_BATCH, n_pages).astype(jnp.int32),
        'meta': nrm(ks[7], (N_META, D_MODEL)),
        'g_attn': 1.0 + 0.02 * nrm(ks[8], (DEPTH, D_MODEL)),
        'g_mlp': 1.0 + 0.02 * nrm(ks[9], (DEPTH, D_MODEL)),
        'w_ret_in': nrm(ks[10], (N_A, D_MODEL, RET_IN_WIDTH), D_MODEL ** -0.5),
        'w_ret_out': nrm(ks[11], (N_A, RET_HEADS * RET_DV, D_MODEL), (RET_HEADS * RET_DV) ** -0.5),
        'g_kv': 1.0 + 0.02 * nrm(ks[12], (D_MODEL,)),
        'w_kvf': nrm(ks[13], (D_MODEL, 2 * D_MODEL + FOX_HEADS), D_MODEL ** -0.5),
        'b_f': jax.random.uniform(ks[14], (FOX_HEADS,), f32, 2.0, 6.0),
        'g_k': 1.0 + 0.02 * nrm(ks[15], (FOX_DH,)),
        'w_fox_qg': nrm(ks[16], (N_B, D_MODEL, 2 * D_MODEL), D_MODEL ** -0.5),
        'g_q': 1.0 + 0.02 * nrm(ks[17], (N_B, FOX_DH)),
        'w_fox_out': nrm(ks[18], (N_B, D_MODEL, D_MODEL), D_MODEL ** -0.5),
        'w_mlp_up': nrm(ks[19], (DEPTH, D_MODEL, D_FF), D_MODEL ** -0.5),
        'w_mlp_down': nrm(ks[20], (DEPTH, D_FF, D_MODEL), D_FF ** -0.5),
    }

def reference(x_prompt, x_sample, state_ret, cache_k, cache_v, cache_logf, page_table, meta, g_attn, g_mlp,
              w_ret_in, w_ret_out, g_kv, w_kvf, b_f, g_k, w_fox_qg, g_q, w_fox_out, w_mlp_up, w_mlp_down):
    y_prompt, state_ret_prompt, k_prompt, v_prompt, logf_prompt = prompt_forward(
        x_prompt, meta, g_attn, g_mlp, w_ret_in, w_ret_out, g_kv, w_kvf, b_f, g_k,
        w_fox_qg, g_q, w_fox_out, w_mlp_up, w_mlp_down)
    y_sample, state_ret_sample, k_sample, v_sample, logf_sample = sample_forward(
        x_sample, state_ret, cache_k, cache_v, cache_logf, page_table, g_attn, g_mlp, w_ret_in,
        w_ret_out, g_kv, w_kvf, b_f, g_k, w_fox_qg, g_q, w_fox_out, w_mlp_up, w_mlp_down)
    return (y_prompt, y_sample, state_ret_prompt, state_ret_sample, k_prompt, v_prompt, logf_prompt,
            k_sample, v_sample, logf_sample)


_drawn_inputs = setup_inputs


def setup_inputs(seed=0):
    import zlib

    import numpy as np

    out = dict(_drawn_inputs(seed))
    spreads = {}
    factors = {'cache_logf': 7.772, 'g_kv': 2.862, 'g_k': 3.017, 'g_q': 8.0}
    for name, (base, spread) in spreads.items():
        noise = np.random.default_rng([zlib.crc32(name.encode()), seed]).standard_normal(out[name].shape)
        drawn = base * np.exp(spread * noise) if base else spread * noise
        out[name] = __import__('jax').numpy.asarray(drawn.astype(out[name].dtype))
    for name, factor in factors.items():
        out[name] = (out[name] * factor).astype(out[name].dtype)
    return out
```

```python
from contextlib import ExitStack

import numpy as np

import concourse.bass as bass
from concourse import mybir

F32 = mybir.dt.float32
F32R = mybir.dt.float32r
I32 = mybir.dt.int32
ALU = mybir.AluOpType
ACT = mybir.ActivationFunctionType
AX = mybir.AxisListType.X

P = 128
D = 1024
KT = D // P
NSAMP, NMETA, NPROMPT = 64, 16, 512
T = NSAMP + NMETA + NPROMPT
HF = T // 2
W0 = NSAMP + NMETA
DB, DS = 8, 8
RH, DK, DV = 4, 256, 512
FH, DH = 16, 64
DFF = 4 * D
PAST, PAGE, NPAGE = 1024, 128, 8
NKEY = NMETA + NPROMPT
SK = PAST + NSAMP
EPS = 1e-6
NEG = -1e30
BW = 256

WINDOWS = [(0, W0)] + [(W0 + P * c, P) for c in range(4)]


def columns(spec):
    at, out = 0, {}
    for name, n in spec:
        out[name] = (at, n)
        at += n
    return out, at


KEEP, KEEP_N = columns([("ident", P), ("ones", P), ("blk", P), ("eps", 1), ("one", 1)])
RET, RET_N = columns([("cos", T), ("sin", T), ("dec", RH * P), ("dec0", RH * W0), ("qdec", RH * P),
                      ("sqdec", RH * NSAMP), ("kdec", RH), ("kdec0", RH * (DB + 1)), ("gC", RH), ("g8", RH)])
FOX, FOX_N = columns([("causal", P), ("newmask", DB * NSAMP), ("own", NSAMP), ("headpick", 4)])
ROW, ROW_N = columns([("negsel", FH * P), ("rep", P)])


def constants():
    f = np.float32
    keep = np.zeros((P, KEEP_N), f)

    def put(dst, where, name, value):
        a, n = where[name]
        v = np.asarray(value, f).reshape(value.shape[0], n)
        dst[:v.shape[0], a:a + n] = v

    put(keep, KEEP, "ident", np.eye(P))
    put(keep, KEEP, "ones", np.ones((P, P)))
    put(keep, KEEP, "blk", np.kron(np.eye(2), np.ones((DH, DH))))
    put(keep, KEEP, "eps", np.full((P, 1), EPS))
    put(keep, KEEP, "one", np.ones((P, 1)))

    ret = np.zeros((P, RET_N), f)
    half = DK // 2
    inv_freq = (10000.0 ** (-np.arange(half, dtype=np.float64) / half)).astype(f)
    pos = np.concatenate([np.tile(PAST + np.arange(DS), DB), np.arange(NMETA + NPROMPT)]).astype(f)
    ang = (pos[None, :] * inv_freq[:, None]).astype(f)
    put(ret, RET, "cos", np.cos(ang.astype(np.float64)))
    put(ret, RET, "sin", np.sin(ang.astype(np.float64)))
    lg = np.log1p(-np.exp2(-5.0 - np.arange(RH)))
    i = np.arange(P)
    kscale = DK ** -0.5
    diff = i[None, :] - i[:, None]
    dec = [np.where(diff >= 0, np.exp(g * np.maximum(diff, 0)), 0) * kscale for g in lg]
    put(ret, RET, "dec", np.stack(dec, 1))
    t = np.arange(W0)
    same = ((t[:, None] // DS == t[None, :] // DS) & (t[:, None] < NSAMP) & (t[None, :] < NSAMP)) | (
        (t[:, None] >= NSAMP) & (t[None, :] >= NSAMP))
    diff0 = t[None, :] - t[:, None]
    dec0 = [np.where(same & (diff0 >= 0), np.exp(g * np.maximum(diff0, 0)), 0) * kscale for g in lg]
    put(ret, RET, "dec0", np.stack(dec0, 1))
    rep = np.ones((P, 1, 1))
    put(ret, RET, "qdec", rep * np.exp(lg[:, None] * (i[None, :] + 1))[None])
    put(ret, RET, "sqdec", rep * np.exp(lg[:, None] * (np.arange(NSAMP)[None, :] % DS + 1))[None])
    put(ret, RET, "kdec", np.exp(lg[None, :] * (P - 1 - i[:, None])) * kscale)
    kd0 = np.zeros((W0, RH, DB + 1))
    for b in range(DB):
        s = slice(DS * b, DS * b + DS)
        kd0[s, :, b] = np.exp(lg[None, :] * (DS - 1 - np.arange(DS)[:, None])) * kscale
    kd0[NSAMP:, :, DB] = np.exp(lg[None, :] * (NMETA - 1 - np.arange(NMETA)[:, None])) * kscale
    put(ret, RET, "kdec0", kd0)
    put(ret, RET, "gC", np.ones((P, 1)) * np.exp(lg * P)[None])
    put(ret, RET, "g8", np.ones((P, 1)) * np.exp(lg * DS)[None])

    fox = np.zeros((P, FOX_N), f)
    put(fox, FOX, "causal", np.where(i[None, :] <= i[:, None], 0.0, NEG))
    hq = np.arange(P)
    j = np.arange(NSAMP)
    nm = np.full((P, DB, NSAMP), NEG)
    for b in range(DB):
        ok = (j[None, :] // DS == b) & (j[None, :] % DS <= hq[:, None] % DS)
        nm[:, b, :][ok] = 0.0
    put(fox, FOX, "newmask", nm)
    put(fox, FOX, "own", (j[None, :] // DS == hq[:, None] // FH) * 1.0)
    sb = np.zeros((P, DB, P))
    for b in range(DB):
        for h in range(FH):
            sb[b * FH + h, b, h * DS:h * DS + DS] = -1.0
    put(fox, FOX, "headpick", (np.arange(4)[None, :] == hq[:, None] // DS % 4) * 1.0)

    row = np.zeros((FH, ROW_N), f)
    ns = np.zeros((FH, FH, P))
    for h in range(FH):
        ns[h, h, :] = -1.0
    put(row, ROW, "negsel", ns)
    put(row, ROW, "rep", (np.arange(P)[None, :] % FH == np.arange(FH)[:, None]) * 1.0)
    return {"c_keep": keep, "c_ret": ret, "c_fox": fox, "c_row": row, "c_selb": sb.reshape(P, DB * P).astype(f)}


class Blk:

    def __init__(self, c, half=0):
        self.c, self.half = c, half

    def __add__(self, j):
        return Blk(self.c + j, self.half)

    @property
    def n(self):
        return self.c + 2 * self.half

    @property
    def slot(self):
        return self.c % 2

    @property
    def uses(self):
        return self.c // 2 + 1 + self.half


class Tally:

    def __init__(self, sem):
        self.sem, self.base, self.k = sem, 0, 0

    def mark(self, ins):
        ins.then_inc(self.sem, 1)
        self.k += 1
        return self.base + self.k

    def enter(self, i, per):
        self.before, self.base, self.k = self.base + self.k, self.base + self.k + per * i, 0

    def leave(self, per, trips):
        assert self.k == per, (self.k, per)
        self.base, self.k = self.before + per * trips, 0


N_RET = 4
N_MLP0 = N_RET + 10 * (RH - 1) + 6
N_KVF = N_MLP0 + 32
N_QG = N_KVF + 9
N_OUT = N_QG + 8
N_MLP1 = N_OUT + 4
N_END = N_MLP1 + 32


def program(nc, io, stop="all"):
    ctx = ExitStack()
    with ctx:
        def sem(name):
            return ctx.enter_context(nc.semaphore(name))

        PS = ctx.enter_context(nc.psum_tensor("PS", [P, 8, 512], F32))
        arena_bytes = 212000 // 32 * 32
        base = (nc.sbuf_base + 31) // 32 * 32
        ctx.enter_context(nc.sbuf_tensor("arena", [P, arena_bytes // 4], F32))

        def place(name, shape, at, dt=F32):
            n = 4
            for s in shape[1:]:
                n *= s
            n = (n + 31) // 32 * 32
            assert at + n <= arena_bytes, (name, at, n)
            return nc.alloc_sbuf_tensor_at(name, shape, dt, offset=base + at), at + n

        X, at = place("X", [P, KT, T], 0)
        WR = []
        WH = []
        WL = []
        for s in range(2):
            t_, at = place(f"w_raw{s}", [P, KT * BW], at)
            WR.append(t_)
        for s in range(2):
            t_, at = place(f"w_hi{s}", [P, KT * BW], at, F32R)
            WH.append(t_)
            t_, at = place(f"w_lo{s}", [P, KT * BW], at, F32R)
            WL.append(t_)
        CK, at = place("c_keep_sb", [P, KEEP_N], at)
        GN, at = place("gains", [P, 5, KT], at)
        GK, at = place("gain_k", [P, 2], at)
        BF, at = place("b_f_sb", [FH, 1], at)
        R0 = at
        XH, at = place("x_hi", [P, KT, T], R0, F32R)
        XL, at = place("x_lo", [P, KT, T], at, F32R)
        R1 = at
        TT, at = place("temps", [P, 2, T], R1)
        RR, at = place("rms", [P, T], at)
        R2 = at

        CR, at = place("c_ret_sb", [P, RET_N], R2)
        Q, at = place("ret_q", [P, 2, T], at)
        K, at = place("ret_k", [P, 2, T], at)
        QD, at = place("ret_q_decayed", [P, 2, T], at)
        V, at = place("ret_v", [P, 5, DV], at)
        G, at = place("ret_gate", [P, 4, T], at)
        O, at = place("ret_o", [P, 4, T], at)
        S, at = place("ret_state", [P, 2, DV], at)
        KM, at = place("k_w0_decayed", [W0, DB + 1, DK], at)
        KD, at = place("k_decayed", [P, 4, DK], at)
        AT, at = place("scores_t", [P, 4, P], at)
        AT0, at = place("scores_t_w0", [W0, W0], at)
        Y0 = at
        YH, at = place("y_hi", [P, 4, T], Y0, F32R)
        YL, at = place("y_lo", [P, 4, T], at, F32R)
        SB = []
        at = Y0
        for s in range(4):
            t_, at = place(f"sample_state{s}", [P, 2, DV], at)
            SB.append(t_)
        XT, _ = place("x_tokens", [P, 5, D], R2 + 12000)

        HH, at = place("hidden_hi", [P, KT, T], R2, F32R)
        HL, at = place("hidden_lo", [P, KT, T], at, F32R)
        HT, at = place("hidden_tmp", [P, 2, 2, HF], at)

        KTT, at = place("fox_k_t", [P, KT, T], R2)
        GG, at = place("fox_gate", [P, KT, T], at)
        VV, at = place("fox_v", [P, 5, D], at)
        TOK0 = at
        TOK, at = place("fox_tok", [P, 5, D], TOK0)
        LF0 = at
        LF, at = place("logf", [FH, T], LF0)
        CU, at = place("cum", [P, NKEY], at)
        CF, at = place("c_fox_sb", [P, FOX_N], at)
        NS0 = at
        NS, at = place("c_row_sb", [P, ROW_N], NS0)
        LS, at = place("sample_logf", [P, NSAMP], at)
        LFO, at = place("logf_tok", [P, 5, FH], at)
        GKB, at = place("gain_k_row", [P, DH], at)
        NM, at = place("neg_max", [P, 4], at)
        SM, at = place("row_sum", [P, 4], at)
        RM, at = place("row_inv", [P, 4], at)
        SS, at = place("sum_squares", [P, 5, FH], at)
        PT1, at = place("page_table_row", [1, DB * NPAGE], at, I32)
        PT2, at = place("page_table_col", [DB * NPAGE, 1], at, I32)
        QT, at = place("fox_q_t", [P, KT, T], R0)
        KR0 = at
        PTS, at = place("probs_t", [P, 2, 4 * P], TOK0 + 12288)
        PP0, at = place("probs0", [P, NKEY], at)
        PTM, at = place("probs_t_meta", [P, 2, P], at)
        PP1, _ = place("probs1", [P, NKEY], LF0)
        PP = [PP0, PP1]
        KR = []
        at = KR0
        for s in range(4):
            t_, at = place(f"k_page{s}", [P, D], at)
            KR.append(t_)
        QB, at = place("q_blocks", [P, 2, 4, 64], at)
        assert at <= R1
        VR = []
        at = TOK0
        for s in range(3):
            t_, at = place(f"v_page{s}", [P, D], at)
            VR.append(t_)
        KP = []
        for s in range(2):
            t_, at = place(f"k_page_t{s}", [P, KT, P], at)
            KP.append(t_)
        PB, at = place("sample_probs", [P, SK], NS0)
        SEL, at = place("c_selb_sb", [P, DB, P], at)
        PSM, _ = place("sample_probs_t", [P, 8, P], LF0)
        CL, at = place("sample_cum", [P, SK], R1)
        PSN, at = place("sample_probs_t_new", [NSAMP, P], at)
        OX, at = place("o_by_head", [P, 4, DH], at)
        OS, at = place("o_tok", [P, DH], at)
        assert at <= R2
        LFP, _ = place("logf_pages", [DB * NPAGE, PAGE * FH], KR0)
        LFK, _ = place("logf_keys", [P, NPAGE, DB, FH], TOK0)
        YO, _ = place("y_tokens", [P, 5, D], R0)

        def ck(name, rows=P):
            a, n = KEEP[name]
            return CK[0:rows, a:a + n]

        def cf(name):
            a, n = FOX[name]
            return CF[:, a:a + n]

        def cr(name):
            a, n = RET[name]
            return CR[:, a:a + n]

        ident = ck("ident")

        const_in = sem("const_in")
        x_tok_in = sem("x_tok_in")
        x_turned = sem("x_turned")
        x_built = sem("x_built")
        raw_in = [sem("raw_in0"), sem("raw_in1")]
        hi_done = sem("hi_done")
        lo_done = sem("lo_done")
        unit_ready = sem("unit_ready")
        evac_done = sem("evac_done")
        dve_step = sem("dve_step")
        act_step = sem("act_step")
        sq_done = sem("sq_done")
        sq_used = sem("sq_used")
        root_done = sem("root_done")
        inv_done = sem("inv_done")
        xn_done = sem("xn_done")
        xhi_done = sem("xhi_done")
        xlo_done = sem("xlo_done")
        rot_done = sem("rot_done")
        sig_done = sem("sig_done")
        at_ready = sem("at_ready")
        at_done = sem("at_done")
        kt_ready = sem("kt_ready")
        kd_done = sem("kd_done")
        km_done = sem("km_done")
        upd_ready = sem("upd_ready")
        s_done = sem("s_done")
        s_stored = sem("s_stored")
        o_ready = sem("o_ready")
        o_evac = sem("o_evac")
        sb_in = [sem(f"sb_in{s}") for s in range(4)]
        supd_ready = sem("supd_ready")
        sb_done = sem("sb_done")
        sb_stored = [sem(f"sb_stored{s}") for s in range(4)]
        osq_done = sem("osq_done")
        osq_used = sem("osq_used")
        oroot_done = sem("oroot_done")
        y_done = sem("y_done")
        yhi_done = sem("yhi_done")
        ylo_done = sem("ylo_done")
        sqh_done = sem("sqh_done")
        hhi_done = sem("hhi_done")
        hlo_done = sem("hlo_done")
        y_out = sem("y_out")
        fox_in = sem("fox_in")
        f_neg = sem("f_neg")
        f_exp = sem("f_exp")
        f_ln = sem("f_ln")
        lf_done = sem("lf_done")
        sqt_done = sem("sqt_done")
        sqt_used = sem("sqt_used")
        hroot_done = sem("hroot_done")
        tok_done = sem("tok_done")
        small_ready = sem("small_ready")
        small_done = sem("small_done")
        tok_turned = sem("tok_turned")
        tok_evac = sem("tok_evac")
        out_stored = sem("out_stored")
        k_stored = sem("k_stored")
        gate_done = sem("gate_done")
        logf_in = sem("logf_in")
        lfk_ready = sem("lfk_ready")
        lfk_done = sem("lfk_done")
        lfc_ready = sem("lfc_ready")
        lfc_done = sem("lfc_done")
        s_ready = sem("s_ready")
        masked = sem("masked")
        mx_done = sem("mx_done")
        ex_done = sem("ex_done")
        inv_row = sem("inv_row")
        pn_done = sem("pn_done")
        pt_ready = sem("pt_ready")
        pt_evac = sem("pt_evac")
        pv_ready = sem("pv_ready")
        pv_evac = sem("pv_evac")
        page_free = sem("page_free")
        k_in = [sem(f"k_in{s}") for s in range(4)]
        v_in = [sem(f"v_in{s}") for s in range(3)]
        k_used = sem("k_used")
        kp_evac = sem("kp_evac")
        sc_used = sem("sc_used")
        v_used = sem("v_used")
        qb_done = sem("qb_done")
        ss_ready = sem("ss_ready")
        smx_done = sem("smx_done")
        sex_done = sem("sex_done")
        spt_ready = sem("spt_ready")
        spt_evac = sem("spt_evac")
        spv_ready = sem("spv_ready")
        os_done = sem("os_done")
        ot_ready = sem("ot_ready")
        ot_done = sem("ot_done")
        sel_in = sem("sel_in")
        fyhi_done = sem("fyhi_done")
        fylo_done = sem("fylo_done")
        yo_ready = sem("yo_ready")
        yo_done = sem("yo_done")

        w_in = io["w_ret_in"].rearrange("a (t p) n -> p (a t) n", p=P)
        w_ro = io["w_ret_out"].rearrange("a (h t p) n -> p (a h) t n", p=P, t=DV // P)
        w_up = [io["w_mlp_up"][l].rearrange("(t p) n -> p t n", p=P) for l in range(2)]
        w_dn = [io["w_mlp_down"][l].rearrange("(c t p) n -> p c t n", p=P, t=KT) for l in range(2)]

        w_kvf = io["w_kvf"].rearrange("(t p) n -> p t n", p=P)
        w_qg = io["w_fox_qg"].rearrange("a (t p) n -> p (a t) n", p=P)
        w_fo = io["w_fox_out"].rearrange("a (t p) n -> p (a t) n", p=P)
        k_pool = io["cache_k"].rearrange("n k h d -> n k (h d)")
        v_pool = io["cache_v"].rearrange("n k h d -> n k (h d)")

        def keys_of(qb):
            return NMETA + P * (qb + 1)

        def norm_full(k):
            return [0, 1, 2, None, 3][k]

        block = ctx.enter_context(nc.Block())

        @block.sync
        def _(sp):
            def weights(n, src, kt=KT, cols=BW):
                sp.wait_ge(lo_done, n.n + 1)
                sp.dma_start(WR[n.slot][:, 0:kt * cols].rearrange("p (t n) -> p t n", t=kt), src) \
                    .then_inc(raw_in[n.slot], 16)

            def qkv(n, h, js=range(4)):
                for j in js:
                    col = [DK * h, RH * DK + DK * h, 2 * RH * DK + DV * h, 2 * RH * DK + DV * h + BW][j]
                    weights(n + j, w_in[:, :, bass.ds(col, BW)])

            def gate(n, h):
                for j in range(2):
                    weights(n + j, w_in[:, :, bass.ds(2 * RH * DK + RH * DV + DV * h + BW * j, BW)])

            def ret_out(n, h, js=range(4)):
                for j in js:
                    weights(n + j, w_ro[:, bass.ds(h, 1), :, BW * j:BW * j + BW].rearrange("p o t n -> p (o t) n"),
                            kt=DV // P)

            def states(h):
                for b in range(DB):
                    if b < 4:
                        sp.wait_ge(unit_ready, 10 * h + 6)
                    else:
                        sp.wait_ge(sb_stored[b % 4], 32 * h + 16)
                    sp.dma_start(SB[b % 4][:], io["state_ret"][0, b, bass.ds(h, 1)]
                                 .rearrange("o (t p) e -> p (o t) e", p=P)).then_inc(sb_in[b % 4], 16)

            sp.dma_start(CK[:], io["c_keep"]).then_inc(const_in, 16)
            sp.dma_start(XT[0:NSAMP, 0, :], io["x_sample"].rearrange("b s d -> (b s) d")).then_inc(x_tok_in, 16)
            sp.dma_start(XT[NSAMP:W0, 0, :], io["meta"]).then_inc(x_tok_in, 16)
            sp.dma_start(XT[:, 1:5, :], io["x_prompt"].rearrange("o (c p) d -> p (o c) d", p=P)) \
                .then_inc(x_tok_in, 16)
            with nc.allow_non_contiguous_dma(reason="the gains, a few KB"):
                for k, g in enumerate((io["g_attn"][0:1], io["g_mlp"][0:1], io["g_kv"].rearrange("(o d) -> o d", o=1),
                                       io["g_attn"][1:2], io["g_mlp"][1:2])):
                    sp.dma_start(GN[:, k, :], g.rearrange("o (t p) -> p (o t)", p=P)).then_inc(const_in, 16)
                for half in range(2):
                    rows = slice(DH * half, DH * half + DH)
                    sp.dma_start(GK[rows, 0:1], io["g_k"].rearrange("(p o) -> p o", o=1)).then_inc(const_in, 16)
                    sp.dma_start(GK[rows, 1:2], io["g_q"].rearrange("o p -> p o")).then_inc(const_in, 16)
                sp.dma_start(BF[:], io["b_f"].rearrange("(p o) -> p o", o=1)).then_inc(const_in, 16)
            sp.dma_start(CR[:], io["c_ret"]).then_inc(const_in, 16)
            qkv(Blk(0), 0)
            with sp.Fori(0, RH - 1) as h:
                n = Blk(N_RET, 5 * h)
                gate(n, h)
                qkv(n + 2, h + 1, (0, 1))
                states(h)
                qkv(n + 2, h + 1, (2, 3))
                ret_out(n + 6, h)
            h, n = RH - 1, Blk(N_RET + 10 * (RH - 1))
            gate(n, h)
            ret_out(n + 2, h, (0, 1))
            states(h)
            ret_out(n + 2, h, (2, 3))

            def mlp(n0, l):
                with sp.Fori(0, 4) as c:
                    n = Blk(n0, 4 * c)
                    for j in range(4):
                        weights(n + j, w_up[l][:, :, bass.ds(D * c + BW * j, BW)])
                    for j in range(4):
                        weights(n + 4 + j, w_dn[l][:, bass.ds(c, 1), :, BW * j:BW * j + BW]
                                .rearrange("p o t n -> p (o t) n"))
            mlp(N_MLP0, 0)
            if stop == "layer0":
                sp.wait_ge(evac_done, N_KVF + 2)
                sp.dma_start(io["dbg"], X[:]).then_inc(y_out, 16)
                sp.wait_ge(y_out, 16)
                return

            n = Blk(N_KVF)
            sp.wait_ge(lo_done, n.n + 1)
            sp.dma_start(WR[n.slot][:].rearrange("p (t n) -> p t n", t=KT)[:, :, 0:FH], w_kvf[:, :, 2 * D:2 * D + FH]) \
                .then_inc(raw_in[n.slot], 16)
            sp.wait_ge(unit_ready, N_KVF + 2)
            sp.dma_start(CF[:], io["c_fox"]).then_inc(fox_in, 16)
            for r in (0, 64):
                sp.dma_start(NS[r:r + FH, :], io["c_row"]).then_inc(fox_in, 16)
            with nc.allow_non_contiguous_dma(reason="the gain of the keys, on every partition"):
                sp.dma_start(GKB[:], io["g_k"].rearrange("(o d) -> o d", o=1).to_broadcast([P, DH])).then_inc(fox_in, 16)
            sp.dma_start(PT1[:], io["page_table"].rearrange("(o b) p -> o (b p)", o=1)).then_inc(fox_in, 16)
            sp.dma_start(PT2[:], io["page_table"].rearrange("b (p o) -> (b p) o", o=1)).then_inc(fox_in, 16)
            with sp.Fori(0, 4) as i:
                weights(Blk(N_KVF + 1, i), w_kvf[:, :, bass.ds(2 * BW * i, BW)])
                weights(Blk(N_KVF + 2, i), w_kvf[:, :, bass.ds(2 * BW * i + BW, BW)])
            with sp.Fori(0, 4) as i:
                weights(Blk(N_QG, i), w_qg[:, :, bass.ds(2 * BW * i, BW)])
                weights(Blk(N_QG + 1, i), w_qg[:, :, bass.ds(2 * BW * i + BW, BW)])
            for j in range(2):
                weights(Blk(N_OUT + j), w_fo[:, :, BW * j:BW * j + BW])
            sp.wait_ge(mx_done, 64)
            sp.dma_start(SEL[:], io["c_selb"].rearrange("p (b n) -> p b n", b=DB)).then_inc(sel_in, 16)
            sp.wait_ge(lfc_done, 2)
            kn, vn = 0, 0
            sp.wait_ge(fox_in, 16 * 6)
            for b in range(DB + 1):
                for half in range(2):
                    if b < DB:
                        for p in range(4 * half, 4 * half + 4):
                            if kn >= 4:
                                sp.wait_ge(k_used, kn - 3)
                            page = sp.value_load(PT1[0:1, NPAGE * b + p:NPAGE * b + p + 1], min_val=0,
                                                 max_val=io["cache_k"].shape[0] - 1)
                            sp.dma_start(KR[kn % 4][:], k_pool[bass.ds(page, 1)].rearrange("o k f -> k (o f)")) \
                                .then_inc(k_in[kn % 4], 16)
                            kn += 1
                    if b > 0 and half == 0:
                        for p in range(NPAGE):
                            if vn == 0:
                                sp.wait_ge(pv_ready, 32)
                            if vn >= 3:
                                sp.wait_ge(v_used, vn - 2)
                            page = sp.value_load(PT1[0:1, NPAGE * (b - 1) + p:NPAGE * (b - 1) + p + 1], min_val=0,
                                                 max_val=io["cache_v"].shape[0] - 1)
                            sp.dma_start(VR[vn % 3][:], v_pool[bass.ds(page, 1)].rearrange("o k f -> k (o f)")) \
                                .then_inc(v_in[vn % 3], 16)
                            vn += 1
            for j in range(2, 4):
                weights(Blk(N_OUT + j), w_fo[:, :, BW * j:BW * j + BW])
            mlp(N_MLP1, 1)
            for w in range(5):
                sp.wait_ge(yo_done, 2 * (w + 1))
                if w == 0:
                    sp.dma_start(io["y_sample"].rearrange("b s d -> (b s) d"), YO[0:NSAMP, 0, :]).then_inc(y_out, 16)
                else:
                    sp.dma_start(io["y_prompt"][0, P * (w - 1):P * w, :], YO[:, w, :]).then_inc(y_out, 16)
            sp.wait_ge(y_out, 16 * 5)

        N_LAST = N_KVF if stop == "layer0" else N_END

        @block.gpsimd
        def _(pool):
            pool.sem_inc(lo_done, 2)

            def split(n):
                pool.wait_ge(hi_done, n.n + 1)
                pool.tensor_tensor(WL[n.slot][:], WR[n.slot][:], WH[n.slot][:].bitcast(F32), ALU.subtract) \
                    .then_inc(lo_done, 1)

            if stop == "layer0":
                with pool.Fori(0, N_LAST // 2) as i:
                    split(Blk(0, i))
                    split(Blk(1, i))
                return
            with pool.Fori(0, (N_OUT + 1) // 2) as i:
                split(Blk(0, i))
                split(Blk(1, i))
            split(Blk(N_OUT + 1))
            pool.wait_ge(fox_in, 16 * 6)
            pool.wait_ge(unit_ready, N_OUT + 2)
            pool.indirect_dma_start(LFP[:], None, io["cache_logf"].rearrange("n k h -> n (k h)"),
                                    bass.IndirectOffsetOnAxis(ap=PT2[:, 0:1], axis=0)).then_inc(logf_in, 16)
            with pool.Fori(0, (N_END - N_OUT - 2) // 2) as i:
                split(Blk(N_OUT + 2, i))
                split(Blk(N_OUT + 3, i))

        @block.tensor
        def _(pe):
            pe.sem_inc(unit_ready, 2)

            def bank(n, m, hf):
                return PS[:, 4 * n.slot + 2 * m + hf, 0:HF]

            def begin(n):
                pe.wait_ge(lo_done, n.n + 3)
                pe.wait_ge(evac_done, n.n + 1)

            def unit(n, xh, xl, kt=KT, late=None):
                begin(n)
                wh, wl = WH[n.slot], WL[n.slot]
                for m in range(2):
                    for hf in range(2):
                        cols = slice(HF * hf, HF * hf + HF)
                        for t in range(kt):
                            if late and t == kt - 2 and m == 0 and hf == 0:
                                late()
                            w = slice(BW * t + P * m, BW * t + P * m + P)
                            o = bank(n, m, hf)
                            pe.matmul(o, wh[:, w], xh[:, t, cols], start=(t == 0), stop=False)
                            pe.matmul(o, wh[:, w], xl[:, t, cols], start=False, stop=False)
                            last = pe.matmul(o, wl[:, w], xh[:, t, cols], start=False, stop=(t == kt - 1))
                last.then_inc(unit_ready, 1)

            def turn(src, first):
                for t in range(KT):
                    if t >= 4:
                        pe.wait_ge(tok_evac, first + t - 3)
                    for w, (a, n) in enumerate(WINDOWS):
                        o = PS[:, 2 * (t % 4), a:a + n] if w < 4 else PS[:, 2 * (t % 4) + 1, 0:P]
                        last = pe.transpose(o, src[0:n, w, P * t:P * t + P], ident[0:n, 0:n])
                    last.then_inc(tok_turned, 1)
                pe.wait_ge(tok_evac, first + KT)

            def unit_tok(n):
                begin(n)
                wh, wl = WH[n.slot], WL[n.slot]
                for w in range(5):
                    a = WINDOWS[w][0]
                    tok = slice(a, a + P)
                    o = PS[:, 4 * n.slot + w // 2, BW * (w % 2):BW * (w % 2) + BW]
                    for t in range(KT):
                        c = slice(BW * t, BW * t + BW)
                        pe.matmul(o, XH[:, t, tok], wh[:, c], start=(t == 0), stop=False)
                        pe.matmul(o, XL[:, t, tok], wh[:, c], start=False, stop=False)
                        last = pe.matmul(o, XH[:, t, tok], wl[:, c], start=False, stop=(t == KT - 1))
                last.then_inc(unit_ready, 1)

            def norm_sum(k, n):
                f = norm_full(k)
                pe.wait_ge(evac_done, n + 2)
                for t in range(KT):
                    pe.wait_ge(sq_done, KT * f + t + 1)
                    for hf in range(2):
                        last = pe.matmul(PS[:, hf, 0:HF], ck("ones"), TT[:, t % 2, HF * hf:HF * hf + HF],
                                         start=(t == 0), stop=(t == KT - 1))
                    last.then_inc(sq_used, 1)

            def normed(k):
                pe.wait_ge(xlo_done, KT * (k + 1))

            pe.wait_ge(const_in, 16 * 12)
            pe.wait_ge(x_tok_in, 48)
            for t in range(KT):
                if t >= 4:
                    pe.wait_ge(x_built, t - 3)
                for w, (a, n) in enumerate(WINDOWS):
                    o = PS[:, 2 * (t % 4), a:a + n] if w < 4 else PS[:, 2 * (t % 4) + 1, 0:P]
                    last = pe.transpose(o, XT[0:n, w, P * t:P * t + P], ident[0:n, 0:n])
                last.then_inc(x_turned, 1)
            pe.wait_ge(x_built, KT)

            def qkv(n):
                unit(n, XH, XL)
                unit(n + 1, XH, XL)
                unit_tok(n + 2)
                unit_tok(n + 3)

            def retention(n, h):
                unit(n, XH, XL)
                unit(n + 1, XH, XL)
                pe.wait_ge(evac_done, n.n + 4)
                pe.wait_ge(rot_done, 2 * h + 2)
                for c in range(4):
                    a = W0 + P * c
                    for d in range(2):
                        pe.matmul(PS[:, 0, P * c:P * c + P], K[:, d, a:a + P], Q[:, d, a:a + P],
                                  start=(d == 0), stop=(d == 1))
                for d in range(2):
                    last = pe.matmul(PS[0:W0, 1, 0:W0], K[:, d, 0:W0], Q[:, d, 0:W0], start=(d == 0), stop=(d == 1))
                last.then_inc(at_ready, 1)
                for c in range(4):
                    a = W0 + P * c
                    for d in range(2):
                        o = DK * (c % 2) + P * d
                        pe.transpose(PS[:, 2 + c // 2, o:o + P], K[:, d, a:a + P], ident)
                for d in range(2):
                    last = pe.transpose(PS[0:W0, 4, P * d:P * d + P], K[:, d, 0:W0], ident)
                last.then_inc(kt_ready, 1)
                pe.wait_ge(km_done, h + 1)
                for d in range(2):
                    last = pe.matmul(PS[:, 6 + d, :], KM[:, DB, P * d:P * d + P], V[0:W0, 0, :], start=True, stop=True)
                last.then_inc(upd_ready, 1)
                pe.wait_ge(at_done, h + 1)
                pe.wait_ge(kd_done, h + 1)
                for c in range(1, 5):
                    a = W0 + P * (c - 1)
                    ob = 4 + c % 2
                    if c > 2:
                        pe.wait_ge(o_evac, 5 * h + c - 2)
                    for v in range(4):
                        pe.matmul(PS[:, ob, P * v:P * v + P], V[:, c, P * v:P * v + P], AT[:, c - 1, :],
                                  start=(v == 0), stop=False, skip_group_check=True)
                    pe.wait_ge(s_done, 5 * h + c)
                    for v in range(4):
                        for d in range(2):
                            last = pe.matmul(PS[:, ob, P * v:P * v + P], S[:, d, P * v:P * v + P], QD[:, d, a:a + P],
                                             start=False, stop=(d == 1), skip_group_check=True)
                    last.then_inc(o_ready, 1)
                    for d in range(2):
                        last = pe.matmul(PS[:, 6 + d, :], KD[:, c - 1, P * d:P * d + P], V[:, c, :],
                                         start=True, stop=True)
                    last.then_inc(upd_ready, 1)
                for v in range(4):
                    pe.matmul(PS[:, 2, W0 * v:W0 * v + W0], V[0:W0, 0, P * v:P * v + P], AT0[:],
                              start=(v == 0), stop=False, skip_group_check=True)
                for b in range(DB):
                    st = SB[b % 4]
                    pe.wait_ge(sb_in[b % 4], 32 * h + 16 * (b // 4 + 1))
                    for v in range(4):
                        for d in range(2):
                            o = W0 * v + DS * b
                            last = pe.matmul(PS[:, 2, o:o + DS], st[:, d, P * v:P * v + P], QD[:, d, DS * b:DS * b + DS],
                                             start=False, stop=(d == 1), skip_group_check=True)
                    if b == DB - 1:
                        last.then_inc(o_ready, 1)
                    if b == 1:
                        pe.wait_ge(s_done, 5 * h + 5)
                    if b >= 2:
                        pe.wait_ge(sb_done, 8 * h + b - 1)
                    bk = 0 if b % 2 == 0 else 6
                    for d in range(2):
                        last = pe.matmul(PS[:, bk + d, :], KM[:, b, P * d:P * d + P], V[0:W0, 0, :],
                                         start=True, stop=True)
                    last.then_inc(supd_ready, 1)
                pe.wait_ge(o_evac, 5 * h + 4)
                for v in range(4):
                    pe.wait_ge(osq_done, 4 * h + v + 1)
                    for hf in range(2):
                        last = pe.matmul(PS[:, 4 + hf, 0:HF], ck("ones"), TT[:, v % 2, HF * hf:HF * hf + HF],
                                         start=(v == 0), stop=(v == 3))
                    last.then_inc(osq_used, 1)
                pe.wait_ge(sb_done, 8 * h + 8)
                pe.wait_ge(oroot_done, h + 1)

            def ret_out(n, h):
                pe.wait_ge(ylo_done, 4 * h + 4)
                for j in range(4):
                    unit(n + j, YH, YL, kt=DV // P)

            norm_sum(0, 0)
            normed(0)
            qkv(Blk(0))
            with pe.Fori(0, RH - 1) as h:
                n = Blk(N_RET, 5 * h)
                retention(n, h)
                qkv(n + 2)
                ret_out(n + 6, h)
            n = Blk(N_RET + 10 * (RH - 1))
            retention(n, RH - 1)
            ret_out(n + 2, RH - 1)

            def mlp(n0, l):
                with pe.Fori(0, 4) as c:
                    n = Blk(n0, 4 * c)
                    for j in range(4):
                        unit(n + j, XH, XL)
                    k = 16 * l + 4 * c
                    pe.wait_ge(hlo_done, k + 3)
                    unit(n + 4, HH, HL, late=lambda: pe.wait_ge(hlo_done, k + 4))
                    for j in range(1, 4):
                        unit(n + 4 + j, HH, HL)
            norm_sum(1, N_MLP0)
            normed(1)
            mlp(N_MLP0, 0)
            if stop == "layer0":
                return

            norm_sum(2, N_KVF)
            normed(2)
            n = Blk(N_KVF)
            begin(n)
            for hf in range(2):
                cols = slice(HF * hf, HF * hf + HF)
                for t in range(KT):
                    w = slice(BW * t, BW * t + P)
                    pe.matmul(bank(n, 0, hf), WH[n.slot][:, w], XH[:, t, cols], start=(t == 0), stop=False)
                    pe.matmul(bank(n, 0, hf), WH[n.slot][:, w], XL[:, t, cols], start=False, stop=False)
                    last = pe.matmul(bank(n, 0, hf), WL[n.slot][:, w], XH[:, t, cols], start=False, stop=(t == KT - 1))
            last.then_inc(unit_ready, 1)
            with pe.Fori(0, 4) as i:
                unit_tok(Blk(N_KVF + 1, i))
                unit_tok(Blk(N_KVF + 2, i))
            pe.wait_ge(fox_in, 16 * 6)
            pe.wait_ge(evac_done, N_QG + 2)
            pe.wait_ge(lf_done, 2)
            for w, (a, n) in enumerate(WINDOWS):
                pe.transpose(PS[0:n, 0, FH * w:FH * w + FH], LF[:, a:a + n], ident[0:FH, 0:FH])
            a, n = ROW["rep"]
            pe.matmul(PS[:, 1, 0:NSAMP], NS[0:FH, a:a + n], LF[:, 0:NSAMP], start=True, stop=True) \
                .then_inc(small_ready, 1)
            pe.wait_ge(small_done, 1)
            pe.wait_ge(tok_done, 5)
            turn(TOK, 0)
            normed(3)
            with pe.Fori(0, 2) as i:
                unit_tok(Blk(N_QG, i))
                unit_tok(Blk(N_QG + 1, i))
            with pe.Fori(0, 2) as i:
                unit(Blk(N_QG + 4, i), XH, XL)
                unit(Blk(N_QG + 5, i), XH, XL)
            pe.wait_ge(evac_done, N_OUT + 2)
            pe.wait_ge(tok_done, 10)
            turn(TOK, KT)

            pe.wait_ge(logf_in, 16)
            for h in range(FH):
                last = pe.transpose(PS[:, h // 8, 64 * (h % 8):64 * (h % 8) + 64],
                                    LFP[:].rearrange("q (k h) -> q k h", h=FH)[:, :, h], ident[0:64, 0:64])
            last.then_inc(lfk_ready, 1)
            pe.wait_ge(lfk_done, 2)
            for p in range(NPAGE):
                last = pe.transpose(PS[:, 2 + p // 4, P * (p % 4):P * (p % 4) + P],
                                    LFK[:, p].rearrange("k b h -> k (b h)"), ident)
            last.then_inc(lfc_ready, 1)
            pe.wait_ge(lfc_done, 2)

            def bank_of(j, par):
                return par if j % 2 == 0 else 2 + 2 * par

            def scores(j):
                t, qb = j // 4, j % 4
                if j >= 2:
                    pe.wait_ge(pv_evac, j - 1)
                q = slice(W0 + P * qb, W0 + P * qb + P)
                pieces = [(0, min(512, keys_of(qb)))] + ([(512, keys_of(qb))] if keys_of(qb) > 512 else [])
                for part in range(2):
                    for i, (a, e) in enumerate(pieces):
                        for par in range(2):
                            o = PS[:, bank_of(j, par) + i, 0:e - a]
                            r = slice(64 * par, 64 * par + FH)
                            d = slice(DH * par, DH * par + DH)
                            if part == 0:
                                last = pe.matmul(o, NS[r, P * (2 * t + par):P * (2 * t + par) + P], CU[r, a:e],
                                                 start=True, stop=False)
                            else:
                                last = pe.matmul(o, QT[d, t, q], KTT[d, t, NSAMP + a:NSAMP + e], start=False, stop=True)
                last.then_inc(s_ready, 1)

            def probs_t(j):
                qb = j % 4
                for par in range(2):
                    pe.wait_ge(pn_done, 2 * j + par + 1)
                    pe.transpose(PS[0:NMETA, bank_of(j, par), 0:P], PP[par][:, 0:NMETA], ident)
                    for kb in range(qb + 1):
                        last = pe.transpose(PS[:, 6 + par, P * kb:P * kb + P],
                                            PP[par][:, NMETA + P * kb:NMETA + P * kb + P], ident)
                    last.then_inc(pt_ready, 1)

            def values(j):
                t, qb = j // 4, j % 4
                pe.wait_ge(pt_evac, 2 * j + 2)
                for par in range(2):
                    h = slice(DH * (2 * t + par), DH * (2 * t + par) + DH)
                    o = PS[DH * par:DH * par + DH, bank_of(j, 0), 256:384]
                    pe.matmul(o, VV[NSAMP:W0, 0, h], PTM[NSAMP:W0, par, :], start=True, stop=False)
                    for kb in range(qb + 1):
                        last = pe.matmul(o, VV[:, 1 + kb, h], PTS[:, par, P * kb:P * kb + P], start=False,
                                         stop=(kb == qb))
                last.then_inc(pv_ready, 1)

            NPAIR = 4 * KT
            scores(0)
            for j in range(NPAIR):
                probs_t(j)
                if j + 1 < NPAIR:
                    scores(j + 1)
                values(j)
            pe.wait_ge(pv_evac, NPAIR)

            slots = [0]

            def slot_begin():
                k = slots[0]
                if k >= 2:
                    pe.wait_ge(kp_evac, k - 1)
                slots[0] += 1
                return 4 + 2 * (k % 2)

            def page_t(b, p):
                kn = NPAGE * b + p
                pe.wait_ge(k_in[kn % 4], 16 * (kn // 4 + 1))
                s = slot_begin()
                for t in range(KT):
                    last = pe.transpose(PS[:, s + t // 4, P * (t % 4):P * (t % 4) + P], KR[kn % 4][:, P * t:P * t + P],
                                        ident)
                last.then_inc(k_used, 1)

            def bias(b):
                if b == 0:
                    pe.wait_ge(sel_in, 16)
                else:
                    pe.wait_ge(sex_done, b)
                for i, (a, e) in enumerate(((0, 512), (512, 1024), (1024, SK))):
                    pe.matmul(PS[:, i, 0:e - a], SEL[:, b, :], CL[:, a:e], start=True, stop=False,
                              skip_group_check=True)

            def q_k(b, o_bank, o_cols, rhs, stop=True):
                for e in range(2):
                    for g in range(4):
                        last = pe.matmul(PS[32 * g:32 * g + 32, o_bank, o_cols], QB[:, b % 2, g, 32 * e:32 * e + 32],
                                         rhs(2 * g + e), start=False, stop=(e == 1), skip_group_check=True)
                return last

            def page_scores(b, p):
                kn = NPAGE * b + p
                pe.wait_ge(kp_evac, copied[p])
                if p == 0:
                    pe.wait_ge(qb_done, b + 1)
                q_k(b, p // 4, slice(P * (p % 4), P * (p % 4) + P), lambda t: KP[kn % 2][:, t, :]).then_inc(sc_used, 1)

            def probs_values(b):
                pe.wait_ge(sex_done, b + 1)
                s = slot_begin()
                for p in range(NPAGE):
                    last = pe.transpose(PS[:, s + p // 4, P * (p % 4):P * (p % 4) + P], PB[:, P * p:P * p + P], ident)
                last.then_inc(spt_ready, 1)
                s = slot_begin()
                pe.transpose(PS[0:NSAMP, s, 0:P], PB[:, PAST:SK], ident).then_inc(spt_ready, 1)
                pe.wait_ge(kp_evac, slots[0])
                if b > 0:
                    pe.wait_ge(ot_done, 2 * b)
                for p in range(NPAGE):
                    vn = NPAGE * b + p
                    pe.wait_ge(v_in[vn % 3], 16 * (vn // 3 + 1))
                    for g in range(4):
                        last = pe.matmul(PS[32 * g:32 * g + 32, 3, 0:256], PSM[:, p, 32 * g:32 * g + 32],
                                         VR[vn % 3][:, 256 * g:256 * g + 256], start=(p == 0), stop=False)
                    last.then_inc(v_used, 1)
                for g in range(4):
                    last = pe.matmul(PS[32 * g:32 * g + 32, 3, 0:256], PSN[:, 32 * g:32 * g + 32],
                                     VV[0:NSAMP, 0, 256 * g:256 * g + 256], start=False, stop=True)
                last.then_inc(spv_ready, 1)

            def out_t(b):
                pe.wait_ge(os_done, b + 1)
                pe.transpose(PS[0:DH, 3, 256:384], OS[:], ident).then_inc(ot_ready, 1)

            copied = {}
            for b in range(DB + 1):
                if b < DB:
                    for p in range(4):
                        page_t(b, p)
                        copied[p] = slots[0]
                        if p == 1:
                            bias(b)
                        if p >= 1:
                            page_scores(b, p - 1)
                    page_scores(b, 3)
                if b > 0:
                    probs_values(b - 1)
                if b < DB:
                    for p in range(4, 8):
                        page_t(b, p)
                        copied[p] = slots[0]
                        if p >= 5:
                            page_scores(b, p - 1)
                    page_scores(b, 7)
                    q_k(b, 2, slice(0, NSAMP), lambda t: KTT[:, t, 0:NSAMP]).then_inc(ss_ready, 1)
                if b > 0:
                    out_t(b - 1)

            pe.wait_ge(fylo_done, KT)
            pe.wait_ge(ot_done, 2 * DB)
            with pe.Fori(0, 2) as i:
                unit(Blk(N_OUT, i), XH, XL)
                unit(Blk(N_OUT + 1, i), XH, XL)
            norm_sum(4, N_MLP1)
            normed(4)
            mlp(N_MLP1, 1)
            pe.wait_ge(evac_done, N_END + 2)
            for w, (a, n) in enumerate(WINDOWS):
                for half in range(2):
                    k = 2 * w + half
                    if k >= 8:
                        pe.wait_ge(yo_done, k - 7)
                    for t in range(4):
                        last = pe.transpose(PS[0:n, k % 8, P * t:P * t + P], X[:, 4 * half + t, a:a + n], ident)
                    last.then_inc(yo_ready, 1)

        @block.scalar
        def _(act):
            def w_hi(n):
                act.wait_ge(raw_in[n.slot], 16 * n.uses)
                act.wait_ge(unit_ready, n.n + 1)
                act.activation(WH[n.slot][:], WR[n.slot][:], ACT.Copy).then_inc(hi_done, 1)

            def norm(k, n):
                f = norm_full(k)
                if f is not None:
                    act.wait_ge(evac_done, n + 2)
                    for t in range(KT):
                        if f > 0 or t >= 2:
                            act.wait_ge(sq_used, KT * f + t - 1)
                        act.activation(TT[:, t % 2, :], X[:, t, :], ACT.Square).then_inc(sq_done, 1)
                    act.wait_ge(sq_used, KT * f + KT)
                    act.activation(RR[:].rearrange("p (a n) -> p a n", a=2), PS[:, 0:2, 0:HF], ACT.Sqrt,
                                   scale=1.0 / D, bias=ck("eps")).then_inc(root_done, 1)
                act.wait_ge(unit_ready, n + 2)
                for t in range(KT):
                    act.wait_ge(xn_done, KT * k + t + 1)
                    act.activation(XH[:, t, :], TT[:, t % 2, :], ACT.Copy).then_inc(xhi_done, 1)

            act.wait_ge(const_in, 16 * 12)
            for t in range(KT):
                act.wait_ge(x_turned, t + 1)
                act.activation(X[:, t, 0:T - P], PS[:, 2 * (t % 4), 0:T - P], ACT.Copy)
                act.activation(X[:, t, T - P:T], PS[:, 2 * (t % 4) + 1, 0:P], ACT.Copy).then_inc(x_built, 1)
            act.wait_ge(x_built, KT)
            norm(0, 0)
            w_hi(Blk(0))
            w_hi(Blk(1))
            for j in range(4):
                w_hi(Blk(2 + j))

            def retention(n, h):
                for j in range(2):
                    m = n + j
                    w_hi(m + 2)
                    act.wait_ge(unit_ready, m.n + 3)
                    for t in range(2):
                        ins = act.activation(G[:, 2 * j + t, :].rearrange("p (a n) -> p a n", a=2),
                                             PS[:, 4 * m.slot + 2 * t:4 * m.slot + 2 * t + 2, 0:HF], ACT.Sigmoid)
                    ins.then_inc(sig_done, 1)
                act.wait_ge(kt_ready, h + 1)
                act.activation(KD[:].rearrange("p c d -> p (c d)"), PS[:, 2:4, :].rearrange("p a n -> p (a n)"),
                               ACT.Copy, scale=cr("kdec")[:, bass.ds(h, 1)]).then_inc(kd_done, 1)
                for c in range(1, 5):
                    a = W0 + P * (c - 1)
                    act.wait_ge(o_ready, 5 * h + c)
                    act.activation(O[:, :, a:a + P], PS[:, 4 + c % 2, :].rearrange("p (v n) -> p v n", v=4), ACT.Copy) \
                        .then_inc(o_evac, 1)
                act.wait_ge(s_done, 5 * h + 5)
                act.dma_start(io["state_ret_prompt"][0, 0, bass.ds(h, 1)].rearrange("o (t p) e -> p (o t) e", p=P),
                              S[:]).then_inc(s_stored, 16)
                for b in range(DB):
                    act.wait_ge(sb_done, 8 * h + b + 1)
                    act.dma_start(io["state_ret_sample"][0, b, bass.ds(h, 1)]
                                  .rearrange("o (t p) e -> p (o t) e", p=P), SB[b % 4][:]) \
                        .then_inc(sb_stored[b % 4], 16)
                act.wait_ge(o_ready, 5 * h + 5)
                act.activation(O[:, :, 0:W0], PS[:, 2, 0:4 * W0].rearrange("p (v n) -> p v n", v=4), ACT.Copy) \
                    .then_inc(o_evac, 1)
                act.wait_ge(o_evac, 5 * h + 5)
                for v in range(4):
                    if v >= 2:
                        act.wait_ge(osq_used, 4 * h + v - 1)
                    act.activation(TT[:, v % 2, :], O[:, v, :], ACT.Square).then_inc(osq_done, 1)
                act.wait_ge(osq_used, 4 * h + 4)
                act.activation(RR[:].rearrange("p (a n) -> p a n", a=2), PS[:, 4:6, 0:HF], ACT.Sqrt,
                               scale=1.0 / DV, bias=ck("eps")).then_inc(oroot_done, 1)
                for s in range(4):
                    act.wait_ge(sb_stored[s], 32 * h + 32)
                for v in range(4):
                    act.wait_ge(y_done, 4 * h + v + 1)
                    act.activation(YH[:, v, :], O[:, v, :], ACT.Copy).then_inc(yhi_done, 1)

            with act.Fori(0, RH - 1) as h:
                n = Blk(N_RET, 5 * h)
                retention(n, h)
                for j in range(8):
                    w_hi(n + 4 + j)
            n = Blk(N_RET + 10 * (RH - 1))
            retention(n, RH - 1)
            for j in range(4):
                w_hi(n + 4 + j)

            def mlp(n0, l, last=8):
                def up(n, k, j):
                    w_hi(n + 2)
                    act.wait_ge(evac_done, n.n + 3)
                    if j == 0:
                        act.wait_ge(unit_ready, n.n + 2)
                    act.activation(HH[:, 2 * j:2 * j + 2, :].rearrange("p m (a n) -> p m a n", a=2),
                                   HT[:], ACT.Square).then_inc(hhi_done, 1)
                with act.Fori(0, 3) as c:
                    n = Blk(n0, 4 * c)
                    for j in range(4):
                        up(n + j, 16 * l + 4 * c, j)
                    for j in range(4):
                        w_hi(n + 4 + j + 2)
                n = Blk(n0 + 24)
                for j in range(4):
                    up(n + j, 16 * l + 12, j)
                for j in range(4):
                    if n.c + 4 + j + 2 < N_LAST:
                        w_hi(n + 4 + j + 2)
            norm(1, N_MLP0)
            act.wait_ge(s_stored, 16 * RH + 16)
            mlp(N_MLP0, 0)
            if stop == "layer0":
                return

            norm(2, N_KVF)
            w_hi(Blk(N_KVF + 2))
            act.wait_ge(f_neg, 1)
            f = TT[0:FH, 1, :]
            act.activation(f, f, ACT.Exp).then_inc(f_exp, 1)
            act.wait_ge(f_exp, 1)
            act.activation(f, f, ACT.Ln, bias=1.0).then_inc(f_ln, 1)

            def by_head(k):
                sq = TT[:].rearrange("p a n -> p (a n)")[:, 0:D]
                for w in range(5):
                    if w == 0:
                        act.wait_ge(evac_done, (N_KVF + 5 if k == 0 else N_QG + 4) + 2)
                    if k or w:
                        act.wait_ge(sqt_used, 5 * k + w)
                    act.activation(sq, TOK[:, w, :], ACT.Square).then_inc(sqt_done, 1)
                act.wait_ge(sqt_used, 5 * k + 5)
                act.activation(SS[:], SS[:], ACT.Sqrt, scale=1.0 / DH, bias=ck("eps")).then_inc(hroot_done, 1)

            def turn(dst, first, scale):
                for t in range(KT):
                    act.wait_ge(tok_turned, first + t + 1)
                    act.activation(dst[:, t, 0:T - P], PS[:, 2 * (t % 4), 0:T - P], ACT.Copy, scale=scale)
                    act.activation(dst[:, t, T - P:T], PS[:, 2 * (t % 4) + 1, 0:P], ACT.Copy, scale=scale) \
                        .then_inc(tok_evac, 1)

            for j in range(4):
                w_hi(Blk(N_KVF + 3 + j))
            by_head(0)
            for j in range(4):
                w_hi(Blk(N_KVF + 7 + j))
            act.wait_ge(evac_done, N_QG + 2)
            out_v = [(io["v_prompt"][0, NMETA:].rearrange("(c p) h d -> p c (h d)", p=P), VV[:, 1:5, :]),
                     (io["v_prompt"][0, 0:NMETA].rearrange("p h d -> p (h d)"), VV[NSAMP:W0, 0, :]),
                     (io["v_sample"].rearrange("b s h d -> (b s) (h d)"), VV[0:NSAMP, 0, :])]
            out_k = [(io["k_prompt"][0, NMETA:].rearrange("(c p) h d -> p c (h d)", p=P), TOK[:, 1:5, :]),
                     (io["k_prompt"][0, 0:NMETA].rearrange("p h d -> p (h d)"), TOK[NSAMP:W0, 0, :]),
                     (io["k_sample"].rearrange("b s h d -> (b s) (h d)"), TOK[0:NSAMP, 0, :])]
            out_f = [(io["logf_prompt"][0, NMETA:].rearrange("(c p) h -> p c h", p=P), LFO[:, 1:5, :]),
                     (io["logf_prompt"][0, 0:NMETA], LFO[NSAMP:W0, 0, :]),
                     (io["logf_sample"].rearrange("b s h -> (b s) h"), LFO[0:NSAMP, 0, :])]
            for dst, src in out_v:
                act.dma_start(dst, src).then_inc(out_stored, 16)
            act.wait_ge(tok_done, 5)
            for dst, src in out_k:
                act.dma_start(dst, src).then_inc(k_stored, 16)
            act.wait_ge(small_done, 1)
            for dst, src in out_f:
                act.dma_start(dst, src).then_inc(out_stored, 16)
            turn(KTT, 0, 1.0)
            act.wait_ge(tok_evac, KT)
            norm(3, N_QG)
            for j in range(4):
                w_hi(Blk(N_QG + 2 + j))
            by_head(1)
            for j in range(4):
                n = Blk(N_QG + 4 + j)
                w_hi(n + 2)
                act.wait_ge(unit_ready, n.n + 3)
                act.activation(GG[:, 2 * j:2 * j + 2, :].rearrange("p m (a n) -> p m a n", a=2),
                               PS[:, 4 * n.slot:4 * n.slot + 4, 0:HF].rearrange("p (m a) n -> p m a n", a=2),
                               ACT.Sigmoid).then_inc(gate_done, 1)
            act.wait_ge(unit_ready, N_OUT + 2)
            turn(QT, KT, GK[:, 1:2])

            def bank_of(j, par):
                return par if j % 2 == 0 else 2 + 2 * par

            for j in range(4 * KT):
                qb = j % 4
                n = keys_of(qb)
                for par in range(2):
                    act.wait_ge(mx_done, 2 * j + par + 1)
                    b = bank_of(j, par)
                    src = PS[:, b:b + 2, :].rearrange("p a n -> p (a n)")[:, 0:n]
                    act.activation(PP[par][:, 0:n], src, ACT.Exp, bias=NM[:, par:par + 1],
                                   accum_out=SM[:, par:par + 1]).then_inc(ex_done, 1)
                for par in range(2):
                    act.wait_ge(pt_ready, 2 * j + par + 1)
                    act.activation(PTM[NSAMP:W0, par, :], PS[0:NMETA, bank_of(j, par), 0:P], ACT.Copy)
                    act.activation(PTS[:, par, 0:P * (qb + 1)], PS[:, 6 + par, 0:P * (qb + 1)], ACT.Copy) \
                        .then_inc(pt_evac, 1)

            def exp_s(b):
                act.wait_ge(smx_done, b + 1)
                act.activation(PB[:], PS[:, 0:3, :].rearrange("p a n -> p (a n)")[:, 0:SK], ACT.Exp, bias=NM[:, 2:3],
                               accum_out=SM[:, 2:3]).then_inc(sex_done, 1)

            def page_copy(b, p, k):
                kn = NPAGE * b + p
                act.wait_ge(k_used, kn + 1)
                if k:
                    act.wait_ge(kp_evac, k)
                if kn >= 2:
                    act.wait_ge(sc_used, kn - 1)
                s = 4 + 2 * (k % 2)
                act.activation(KP[kn % 2][:], PS[:, s:s + 2, :].rearrange("p a (t n) -> p (a t) n", n=P),
                               ACT.Copy).then_inc(kp_evac, 1)

            def probs_copy(b, k):
                act.wait_ge(spt_ready, 2 * b + 1)
                s = 4 + 2 * (k % 2)
                act.activation(PSM[:], PS[:, s:s + 2, :].rearrange("p a (t n) -> p (a t) n", n=P), ACT.Copy) \
                    .then_inc(kp_evac, 1)
                act.wait_ge(spt_ready, 2 * b + 2)
                s = 4 + 2 * ((k + 1) % 2)
                act.activation(PSN[:], PS[0:NSAMP, s, 0:P], ACT.Copy).then_inc(kp_evac, 1)

            k = 0
            for b in range(DB + 1):
                for half in range(2):
                    if b < DB:
                        for p in range(4 * half, 4 * half + 4):
                            if b and p == 1:
                                exp_s(b - 1)
                            page_copy(b, p, k)
                            k += 1
                    elif half == 0:
                        exp_s(b - 1)
                    if b and half == 0:
                        probs_copy(b - 1, k)
                        k += 2

            act.wait_ge(ot_done, 2 * DB)
            for t in range(KT):
                act.activation(XH[:, t, :], GG[:, t, :], ACT.Copy).then_inc(fyhi_done, 1)
            for j in range(4):
                w_hi(Blk(N_OUT + 2 + j))
            norm(4, N_MLP1)
            mlp(N_MLP1, 1)
            for k in range(10):
                n = WINDOWS[k // 2][1]
                act.wait_ge(yo_ready, k + 1)
                act.activation(YO[0:n, k // 2, 512 * (k % 2):512 * (k % 2) + 512], PS[0:n, k % 8, :], ACT.Copy) \
                    .then_inc(yo_done, 1)
            act.wait_ge(out_stored, 16 * 6)

        @block.vector
        def _(dve):
            dve.sem_inc(evac_done, 2)
            dve.sem_inc(s_stored, 16)
            step = Tally(dve_step)

            def do(ins):
                dve.wait_ge(dve_step, step.mark(ins))

            def norm(k):
                f = norm_full(k)
                if f is not None:
                    dve.wait_ge(root_done, f + 1)
                    dve.reciprocal(RR[:], RR[:]).then_inc(inv_done, 1)
                    dve.wait_ge(inv_done, f + 1)

                def low(t):
                    dve.wait_ge(xhi_done, KT * k + t + 1)
                    dve.tensor_tensor(XL[:, t, :], TT[:, t % 2, :], XH[:, t, :].bitcast(F32), ALU.subtract) \
                        .then_inc(xlo_done, 1)

                for t in range(KT):
                    if t >= 2:
                        low(t - 2)
                        dve.wait_ge(xlo_done, KT * k + t - 1)
                    dve.scalar_tensor_tensor(TT[:, t % 2, :], X[:, t, :], GN[:, k, t:t + 1], RR[:], ALU.mult,
                                             ALU.mult).then_inc(xn_done, 1)
                low(KT - 2)
                low(KT - 1)
                dve.wait_ge(xlo_done, KT * (k + 1))

            def halves(x):
                return x.rearrange("p (a n) -> p a n", a=2)

            def begin(n):
                dve.wait_ge(unit_ready, n.n + 3)
                dve.wait_ge(evac_done, n.n + 2)

            def rotate(n, dst, last_on_rot):
                begin(n)
                x1, x2 = (PS[:, 4 * n.slot + 2 * m:4 * n.slot + 2 * m + 2, 0:HF] for m in range(2))
                cos, sin = halves(cr("cos")), halves(cr("sin"))
                t1, t2 = halves(TT[:, 0, :]), halves(TT[:, 1, :])
                step.mark(dve.tensor_tensor(t1, x1, cos, ALU.mult))
                do(dve.tensor_tensor(t2, x2, sin, ALU.mult))
                do(dve.tensor_tensor(dst[:, 0, :], TT[:, 0, :], TT[:, 1, :], ALU.subtract))
                step.mark(dve.tensor_tensor(t1, x2, cos, ALU.mult))
                dve.tensor_tensor(t2, x1, sin, ALU.mult).then_inc(evac_done, 1)
                dve.wait_ge(evac_done, n.n + 3)
                ins = dve.tensor_tensor(dst[:, 1, :], TT[:, 0, :], TT[:, 1, :], ALU.add)
                if last_on_rot:
                    ins.then_inc(rot_done, 1)
                else:
                    do(ins)

            def qkv(n, h):
                rotate(n, Q, False)
                for d in range(2):
                    q4 = Q[:, d, W0:T].rearrange("p (c n) -> p c n", c=4)
                    o4 = QD[:, d, W0:T].rearrange("p (c n) -> p c n", c=4)
                    g = cr("qdec")[:, bass.ds(P * h, P)].rearrange("p (o n) -> p o n", o=1).to_broadcast([P, 4, P])
                    dve.tensor_tensor(o4, q4, g, ALU.mult)
                g = cr("sqdec")[:, bass.ds(NSAMP * h, NSAMP)].rearrange("p (o n) -> p o n", o=1) \
                    .to_broadcast([P, 2, NSAMP])
                dve.tensor_tensor(QD[:, :, 0:NSAMP], Q[:, :, 0:NSAMP], g, ALU.mult).then_inc(rot_done, 1)
                rotate(n + 1, K, True)
                for j in range(2):
                    m = n + 2 + j
                    begin(m)
                    dve.tensor_copy(V[:, 0:4, BW * j:BW * j + BW].rearrange("p (a b) n -> p a b n", b=2),
                                    PS[:, 4 * m.slot:4 * m.slot + 2, :].rearrange("p a (b n) -> p a b n", b=2))
                    dve.tensor_copy(V[:, 4, BW * j:BW * j + BW], PS[:, 4 * m.slot + 2, 0:BW]).then_inc(evac_done, 1)

            def retention(n, h):
                for j in range(2):
                    m = n + j
                    begin(m)
                    dve.wait_ge(sig_done, 2 * h + j + 1)
                    g = G[:, 2 * j:2 * j + 2, :].rearrange("p m (a n) -> p m a n", a=2)
                    src = PS[:, 4 * m.slot:4 * m.slot + 4, 0:HF].rearrange("p (m a) n -> p m a n", a=2)
                    dve.tensor_tensor(g, src, g, ALU.mult).then_inc(evac_done, 1)
                dve.wait_ge(at_ready, h + 1)
                g = cr("dec")[:, bass.ds(P * h, P)].rearrange("p (o n) -> p o n", o=1).to_broadcast([P, 4, P])
                dve.tensor_tensor(AT[:], PS[:, 0, :].rearrange("p (c n) -> p c n", c=4), g, ALU.mult)
                dve.tensor_tensor(AT0[:], PS[0:W0, 1, 0:W0], CR[0:W0, bass.ds(W0 * h + RET["dec0"][0], W0)],
                                  ALU.mult).then_inc(at_done, 1)
                dve.wait_ge(kt_ready, h + 1)
                src = PS[0:W0, 4, 0:DK].rearrange("p (o n) -> p o n", o=1).to_broadcast([W0, DB + 1, DK])
                g = CR[0:W0, bass.ds((DB + 1) * h + RET["kdec0"][0], DB + 1)] \
                    .rearrange("p (b o) -> p b o", o=1).to_broadcast([W0, DB + 1, DK])
                dve.tensor_tensor(KM[:], src, g, ALU.mult).then_inc(km_done, 1)
                up = PS[:, 6:8, :]
                dve.wait_ge(upd_ready, 5 * h + 1)
                dve.wait_ge(s_stored, 16 * h + 16)
                dve.tensor_copy(S[:], up).then_inc(s_done, 1)
                for c in range(1, 5):
                    dve.wait_ge(upd_ready, 5 * h + c + 1)
                    dve.wait_ge(s_done, 5 * h + c)
                    dve.scalar_tensor_tensor(S[:], S[:], cr("gC")[:, bass.ds(h, 1)], up, ALU.mult, ALU.add) \
                        .then_inc(s_done, 1)
                for b in range(DB):
                    bk = 0 if b % 2 == 0 else 6
                    dve.wait_ge(supd_ready, 8 * h + b + 1)
                    dve.scalar_tensor_tensor(SB[b % 4][:], SB[b % 4][:], cr("g8")[:, bass.ds(h, 1)],
                                             PS[:, bk:bk + 2, :], ALU.mult, ALU.add).then_inc(sb_done, 1)
                dve.wait_ge(oroot_done, h + 1)
                do(dve.reciprocal(RR[:], RR[:]))
                for v in range(4):
                    do(dve.tensor_tensor(O[:, v, :], O[:, v, :], RR[:], ALU.mult))
                    dve.tensor_tensor(O[:, v, :], O[:, v, :], G[:, v, :], ALU.mult).then_inc(y_done, 1)
                for v in range(4):
                    dve.wait_ge(yhi_done, 4 * h + v + 1)
                    dve.tensor_tensor(YL[:, v, :], O[:, v, :], YH[:, v, :].bitcast(F32), ALU.subtract) \
                        .then_inc(ylo_done, 1)
                dve.wait_ge(ylo_done, 4 * h + 4)

            def residual(n, j):
                begin(n)
                x = X[:, 2 * j:2 * j + 2, :].rearrange("p m (a n) -> p m a n", a=2)
                src = PS[:, 4 * n.slot:4 * n.slot + 4, 0:HF].rearrange("p (m a) n -> p m a n", a=2)
                dve.tensor_tensor(x, src, x, ALU.add).then_inc(evac_done, 1)

            norm(0)
            qkv(Blk(0), 0)
            PER_HEAD = 14
            with dve.Fori(0, RH - 1) as h:
                step.enter(h, PER_HEAD)
                n = Blk(N_RET, 5 * h)
                retention(n, h)
                qkv(n + 2, h + 1)
                for j in range(4):
                    residual(n + 6 + j, j)
            step.leave(PER_HEAD, RH - 1)
            n = Blk(N_RET + 10 * (RH - 1))
            retention(n, RH - 1)
            for j in range(4):
                residual(n + 2 + j, j)

            def mlp(n0, l):
                with dve.Fori(0, 4) as c:
                    n = Blk(n0, 4 * c)
                    k = 16 * l + 4 * c
                    for j in range(4):
                        m = n + j
                        begin(m)
                        if j:
                            dve.wait_ge(hhi_done, k + j)
                            dve.wait_ge(hlo_done, k + j)
                        src = PS[:, 4 * m.slot:4 * m.slot + 4, 0:HF].rearrange("p (m a) n -> p m a n", a=2)
                        dve.tensor_scalar(HT[:], src, 0.0, None, ALU.max).then_inc(evac_done, 1)
                        lo = HL[:, 2 * j:2 * j + 2, :].rearrange("p m (a n) -> p m a n", a=2)
                        hi = HH[:, 2 * j:2 * j + 2, :].bitcast(F32).rearrange("p m (a n) -> p m a n", a=2)
                        dve.wait_ge(hhi_done, k + j + 1)
                        dve.tensor_tensor(HT[:], HT[:], HT[:], ALU.mult).then_inc(sqh_done, 1)
                        dve.wait_ge(sqh_done, k + j + 1)
                        dve.tensor_tensor(lo, HT[:], hi, ALU.subtract).then_inc(hlo_done, 1)
                    for j in range(4):
                        residual(n + 4 + j, j)
            norm(1)
            dve.wait_ge(s_stored, 16 * RH + 16)
            mlp(N_MLP0, 0)
            if stop == "layer0":
                return

            norm(2)
            n = Blk(N_KVF)
            begin(n)
            f0, f1 = TT[0:FH, 0, :], TT[0:FH, 1, :]
            dve.tensor_scalar(halves(f0), PS[0:FH, 4 * n.slot:4 * n.slot + 2, 0:HF], BF[:], None, ALU.add) \
                .then_inc(evac_done, 1)
            dve.wait_ge(evac_done, n.n + 3)
            dve.scalar_tensor_tensor(f1, f0, -1.0, f0, ALU.mult, ALU.min).then_inc(f_neg, 1)
            dve.wait_ge(f_ln, 1)
            dve.scalar_tensor_tensor(LF[:], f0, 0.0, f1, ALU.min, ALU.subtract).then_inc(lf_done, 1)
            dve.wait_ge(lf_done, 1)
            ones = ck("one")
            do(dve.tensor_tensor_scan(CU[0:FH, :], ones[0:FH].to_broadcast([FH, NKEY]), LF[:, NSAMP:T], 0.0, ALU.mult,
                                      ALU.add))
            dve.tensor_copy(CU[64:64 + FH, :], CU[0:FH, :]).then_inc(lf_done, 1)

            def evac_tok(n, dst, j):
                begin(n)
                c = slice(BW * j, BW * j + BW)
                dve.tensor_copy(dst[:, 0:4, c].rearrange("p (a b) n -> p a b n", b=2),
                                PS[:, 4 * n.slot:4 * n.slot + 2, :].rearrange("p a (b n) -> p a b n", b=2))
                dve.tensor_copy(dst[:, 4, c], PS[:, 4 * n.slot + 2, 0:BW]).then_inc(evac_done, 1)

            def by_head(k, gain):
                sq = TT[:].rearrange("p a n -> p (a n)")[:, 0:D].rearrange("p (h d) -> p h d", d=DH)
                for w in range(5):
                    dve.wait_ge(sqt_done, 5 * k + w + 1)
                    dve.reduce_sum(SS[:, w, :], sq, AX).then_inc(sqt_used, 1)
                dve.wait_ge(hroot_done, k + 1)
                do(dve.reciprocal(SS[:], SS[:]))
                for w in range(5):
                    x = TOK[:, w, :].rearrange("p (h d) -> p h d", d=DH)
                    r = SS[:, w, :].rearrange("p (h o) -> p h o", o=1).to_broadcast([P, FH, DH])
                    ins = dve.tensor_tensor(x, x, r, ALU.mult)
                    if gain is not None:
                        do(ins)
                        g = gain.rearrange("p (o d) -> p o d", o=1).to_broadcast([P, FH, DH])
                        ins = dve.tensor_tensor(x, x, g, ALU.mult)
                    ins.then_inc(tok_done, 1)

            for j in range(4):
                evac_tok(Blk(N_KVF + 1 + j), TOK, j)
            dve.wait_ge(fox_in, 16 * 6)
            by_head(0, GKB[:])
            do(dve.tensor_scalar(GK[:, 1:2], GK[:, 1:2], DH ** -0.5, None, ALU.mult))
            for j in range(4):
                evac_tok(Blk(N_KVF + 5 + j), VV, j)
            dve.wait_ge(small_ready, 1)
            dve.tensor_copy(LFO[0:W0, 0, :], PS[0:W0, 0, 0:FH])
            dve.tensor_copy(LFO[:, 1:5, :], PS[:, 0, FH:5 * FH].rearrange("p (w h) -> p w h", h=FH))
            dve.tensor_tensor(LS[:], PS[:, 1, 0:NSAMP], cf("own"), ALU.mult).then_inc(small_done, 1)
            norm(3)
            dve.wait_ge(k_stored, 48)
            dve.wait_ge(tok_evac, KT)
            for j in range(4):
                evac_tok(Blk(N_QG + j), TOK, j)
            by_head(1, None)
            for j in range(4):
                dve.wait_ge(gate_done, j + 1)
                dve.sem_inc(evac_done, 1)
            dve.wait_ge(lfk_ready, 1)
            for i in range(2):
                dve.tensor_copy(LFK[:].rearrange("k p b h -> k h b p")[:, 8 * i:8 * i + 8],
                                PS[:, i, :].rearrange("k (h b p) -> k h b p", h=8, b=DB)).then_inc(lfk_done, 1)
            dve.wait_ge(lfc_ready, 1)
            dve.tensor_tensor_scan(CL[:, 0:PAST], ones.to_broadcast([P, PAST]),
                                   PS[:, 2:4, :].rearrange("p a n -> p (a n)"), 0.0, ALU.mult, ALU.add) \
                .then_inc(lfc_done, 1)
            dve.wait_ge(lfc_done, 1)
            dve.tensor_tensor_scan(CL[:, PAST:SK], ones.to_broadcast([P, NSAMP]), LS[:], CL[:, PAST - 1:PAST],
                                   ALU.mult, ALU.add).then_inc(lfc_done, 1)

            def bank_of(j, par):
                return par if j % 2 == 0 else 2 + 2 * par

            def maxima(j):
                n = keys_of(j % 4)
                dve.wait_ge(s_ready, j + 1)
                for par in range(2):
                    b = bank_of(j, par)
                    flat = PS[:, b:b + 2, :].rearrange("p a n -> p (a n)")
                    dve.tensor_tensor(flat[:, n - P:n], flat[:, n - P:n], cf("causal"), ALU.add).then_inc(masked, 1)
                for par in range(2):
                    b = bank_of(j, par)
                    flat = PS[:, b:b + 2, :].rearrange("p a n -> p (a n)")
                    dve.wait_ge(masked, 2 * j + par + 1)
                    dve.tensor_reduce(NM[:, par:par + 1], flat[:, 0:n], AX, ALU.max, negate=True).then_inc(mx_done, 1)

            def gated(j):
                t, qb = j // 4, j % 4
                dve.wait_ge(pv_ready, j + 1)
                g = GG[:, t, W0 + P * qb:W0 + P * qb + P]
                dve.tensor_tensor(g, PS[:, bank_of(j, 0), 256:384], g, ALU.mult).then_inc(pv_evac, 1)

            def normed_probs(j):
                n = keys_of(j % 4)
                for par in range(2):
                    dve.wait_ge(ex_done, 2 * j + par + 1)
                    dve.reciprocal(RM[:, par:par + 1], SM[:, par:par + 1]).then_inc(inv_row, 1)
                for par in range(2):
                    dve.wait_ge(inv_row, 2 * j + par + 1)
                    dve.tensor_scalar(PP[par][:, 0:n], PP[par][:, 0:n], RM[:, par:par + 1], None, ALU.mult) \
                        .then_inc(pn_done, 1)

            for j in range(4 * KT):
                maxima(j)
                if j:
                    gated(j - 1)
                normed_probs(j)
            gated(4 * KT - 1)

            do(dve.memset(QB[:], 0.0))

            def queries(b):
                if b >= 2:
                    dve.wait_ge(ss_ready, b - 1)
                for par in range(2):
                    r = slice(DH * par, DH * par + DH)
                    for e in range(2):
                        a = 48 * e + DS * par
                        q = QT[r].rearrange("p (g e) n -> p g e n", e=2)[:, :, e, DS * b:DS * b + DS]
                        ins = dve.tensor_copy(QB[r, b % 2, :, a:a + DS], q)
                ins.then_inc(qb_done, 1)

            def maxima_s(b):
                dve.wait_ge(ss_ready, b + 1)
                m = cf("newmask")[:, NSAMP * b:NSAMP * b + NSAMP]
                do(dve.tensor_tensor(PS[:, 2, 0:NSAMP], PS[:, 2, 0:NSAMP], m, ALU.add))
                dve.tensor_reduce(NM[:, 2:3], PS[:, 0:3, :].rearrange("p a n -> p (a n)")[:, 0:SK], AX, ALU.max,
                                  negate=True).then_inc(smx_done, 1)

            def output_s(b):
                dve.wait_ge(spv_ready, b + 1)
                dve.wait_ge(sex_done, b + 1)
                pick = cf("headpick").rearrange("p (h o) -> p h o", o=1).to_broadcast([P, 4, DH])
                do(dve.reciprocal(RM[:, 2:3], SM[:, 2:3]))
                do(dve.tensor_tensor(OX[:], PS[:, 3, 0:256].rearrange("p (h d) -> p h d", d=DH), pick, ALU.mult))
                do(dve.reduce_sum(OS[:], OX[:].rearrange("p h d -> p d h"), AX))
                dve.tensor_scalar(OS[:], OS[:], RM[:, 2:3], None, ALU.mult).then_inc(os_done, 1)

            def gated_s(b):
                dve.wait_ge(ot_ready, b + 1)
                for par in range(2):
                    r = slice(DH * par, DH * par + DH)
                    g = GG[r, :, DS * b:DS * b + DS]
                    o = PS[0:DH, 3, 256:384].rearrange("p (t c q) -> p t c q", c=2, q=DS)[:, :, par, :]
                    dve.tensor_tensor(g, o, g, ALU.mult).then_inc(ot_done, 1)

            queries(0)
            for b in range(DB):
                if b + 1 < DB:
                    queries(b + 1)
                if b:
                    output_s(b - 1)
                maxima_s(b)
                if b:
                    gated_s(b - 1)
            output_s(DB - 1)
            gated_s(DB - 1)

            for t in range(KT):
                dve.wait_ge(fyhi_done, t + 1)
                dve.tensor_tensor(XL[:, t, :], GG[:, t, :], XH[:, t, :].bitcast(F32), ALU.subtract) \
                    .then_inc(fylo_done, 1)
            for j in range(4):
                residual(Blk(N_OUT + j), j)
            norm(4)
            mlp(N_MLP1, 1)


_INS = ["x_prompt", "x_sample", "state_ret", "cache_k", "cache_v", "cache_logf", "page_table", "meta", "g_attn", "g_mlp",
        "w_ret_in", "w_ret_out", "g_kv", "w_kvf", "b_f", "g_k", "w_fox_qg", "g_q", "w_fox_out", "w_mlp_up",
        "w_mlp_down"]
_OUTS = [("y_prompt", (1, NPROMPT, D)), ("y_sample", (DB, DS, D)), ("state_ret_prompt", (1, 1, RH, DK, DV)),
         ("state_ret_sample", (1, DB, RH, DK, DV)), ("k_prompt", (1, NKEY, FH, DH)), ("v_prompt", (1, NKEY, FH, DH)),
         ("logf_prompt", (1, NKEY, FH)), ("k_sample", (DB, DS, FH, DH)), ("v_sample", (DB, DS, FH, DH)),
         ("logf_sample", (DB, DS, FH))]


def build(nc, arrays, stop="all"):
    io = {}
    for name, a in arrays.items():
        io[name] = nc.dram_tensor(f"in_{name}", a.shape, mybir.dt.from_np(a.dtype), kind="ExternalInput").ap()
    for name, shape in _OUTS:
        io[name] = nc.dram_tensor(f"out_{name}", shape, F32, kind="ExternalOutput").ap()
    if stop != "all":
        io["dbg"] = nc.dram_tensor("dbg", (P, KT, T), F32, kind="ExternalOutput").ap()
    program(nc, io, stop)


def kernel(**inputs):
    import concourse.bacc as bacc
    from concourse.bass_utils import run_bass_kernel_spmd

    arrays = {name: np.ascontiguousarray(inputs[name]) for name in _INS}
    arrays.update(constants())
    nc = bacc.Bacc("TRN2", target_bir_lowering=False, num_devices=1)
    build(nc, arrays)
    r = run_bass_kernel_spmd(nc, [{f"in_{k}": v for k, v in arrays.items()}], core_ids=[0])
    return tuple(r.results[0][f"out_{name}"] for name, _ in _OUTS)
```

```python
from contextlib import ExitStack

import numpy as np

import concourse.bass as bass
from concourse import mybir

F32 = mybir.dt.float32
F32R = mybir.dt.float32r
I32 = mybir.dt.int32
ALU = mybir.AluOpType
ACT = mybir.ActivationFunctionType
AX = mybir.AxisListType.X

P = 128
D = 1024
KT = D // P
NSAMP, NMETA, NPROMPT = 64, 16, 512
T = NSAMP + NMETA + NPROMPT
HF = T // 2
W0 = NSAMP + NMETA
DB, DS = 8, 8
RH, DK, DV = 4, 256, 512
FH, DH = 16, 64
DFF = 4 * D
PAST, PAGE, NPAGE = 1024, 128, 8
NKEY = NMETA + NPROMPT
SK = PAST + NSAMP
EPS = 1e-6
NEG = -1e30
BW = 256
NKS, NVS = 5, 5

WINDOWS = [(0, W0)] + [(W0 + P * c, P) for c in range(4)]


def columns(spec):
    at, out = 0, {}
    for name, n in spec:
        out[name] = (at, n)
        at += n
    return out, at


KEEP, KEEP_N = columns([("ident", P), ("ones", P), ("blk", P), ("eps", 1), ("one", 1)])
RET, RET_N = columns([("cos", T), ("sin", T), ("dec", RH * P), ("dec0", RH * W0), ("qdec", RH * P),
                      ("sqdec", RH * NSAMP), ("kdec", RH), ("kdec0", RH * (DB + 1)), ("gC", RH), ("g8", RH),
                      ("own_q", 32)])
FOX, FOX_N = columns([("causal", P), ("newmask", DB * NSAMP), ("own", NSAMP), ("headpick", 4)])
ROW, ROW_N = columns([("negsel", FH * P), ("rep", P)])


def constants():
    f = np.float32
    keep = np.zeros((P, KEEP_N), f)

    def put(dst, where, name, value):
        a, n = where[name]
        v = np.asarray(value, f).reshape(value.shape[0], n)
        dst[:v.shape[0], a:a + n] = v

    put(keep, KEEP, "ident", np.eye(P))
    put(keep, KEEP, "ones", np.ones((P, P)))
    put(keep, KEEP, "blk", np.kron(np.eye(2), np.ones((DH, DH))))
    put(keep, KEEP, "eps", np.full((P, 1), EPS))
    put(keep, KEEP, "one", np.ones((P, 1)))

    ret = np.zeros((P, RET_N), f)
    half = DK // 2
    inv_freq = (10000.0 ** (-np.arange(half, dtype=np.float64) / half)).astype(f)
    pos = np.concatenate([np.tile(PAST + np.arange(DS), DB), np.arange(NMETA + NPROMPT)]).astype(f)
    ang = (pos[None, :] * inv_freq[:, None]).astype(f)
    put(ret, RET, "cos", np.cos(ang.astype(np.float64)))
    put(ret, RET, "sin", np.sin(ang.astype(np.float64)))
    lg = np.log1p(-np.exp2(-5.0 - np.arange(RH)))
    i = np.arange(P)
    kscale = DK ** -0.5
    diff = i[None, :] - i[:, None]
    dec = [np.where(diff >= 0, np.exp(g * np.maximum(diff, 0)), 0) * kscale for g in lg]
    put(ret, RET, "dec", np.stack(dec, 1))
    t = np.arange(W0)
    same = ((t[:, None] // DS == t[None, :] // DS) & (t[:, None] < NSAMP) & (t[None, :] < NSAMP)) | (
        (t[:, None] >= NSAMP) & (t[None, :] >= NSAMP))
    diff0 = t[None, :] - t[:, None]
    dec0 = [np.where(same & (diff0 >= 0), np.exp(g * np.maximum(diff0, 0)), 0) * kscale for g in lg]
    put(ret, RET, "dec0", np.stack(dec0, 1))
    rep = np.ones((P, 1, 1))
    put(ret, RET, "qdec", rep * np.exp(lg[:, None] * (i[None, :] + 1))[None])
    put(ret, RET, "sqdec", rep * np.exp(lg[:, None] * (np.arange(NSAMP)[None, :] % DS + 1))[None])
    put(ret, RET, "kdec", np.exp(lg[None, :] * (P - 1 - i[:, None])) * kscale)
    kd0 = np.zeros((W0, RH, DB + 1))
    for b in range(DB):
        s = slice(DS * b, DS * b + DS)
        kd0[s, :, b] = np.exp(lg[None, :] * (DS - 1 - np.arange(DS)[:, None])) * kscale
    kd0[NSAMP:, :, DB] = np.exp(lg[None, :] * (NMETA - 1 - np.arange(NMETA)[:, None])) * kscale
    put(ret, RET, "kdec0", kd0)
    put(ret, RET, "gC", np.ones((P, 1)) * np.exp(lg * P)[None])
    put(ret, RET, "g8", np.ones((P, 1)) * np.exp(lg * DS)[None])

    r, c = np.arange(P)[:, None], np.arange(32)[None, :]
    put(ret, RET, "own_q", ((r % 32 == c) & (r // 32 == c // DS)) * 1.0)

    fox = np.zeros((P, FOX_N), f)
    put(fox, FOX, "causal", np.where(i[None, :] <= i[:, None], 0.0, NEG))
    hq = np.arange(P)
    j = np.arange(NSAMP)
    nm = np.full((P, DB, NSAMP), NEG)
    for b in range(DB):
        ok = (j[None, :] // DS == b) & (j[None, :] % DS <= hq[:, None] % DS)
        nm[:, b, :][ok] = 0.0
    put(fox, FOX, "newmask", nm)
    put(fox, FOX, "own", (j[None, :] // DS == hq[:, None] // FH) * 1.0)
    sb = np.zeros((P, DB, P))
    for b in range(DB):
        for h in range(FH):
            sb[b * FH + h, b, h * DS:h * DS + DS] = -1.0
    put(fox, FOX, "headpick", (np.arange(4)[None, :] == hq[:, None] // DS % 4) * 1.0)

    row = np.zeros((P, ROW_N), f)
    ns = np.zeros((P, FH, P))
    for h in range(FH):
        ns[[h, 32 + h], h, :] = -1.0
    put(row, ROW, "negsel", ns)
    put(row, ROW, "rep", (np.arange(P)[None, :] % FH == np.arange(FH)[:, None]) * 1.0)
    return {"c_keep": keep, "c_ret": ret, "c_fox": fox, "c_row": row, "c_selb": sb.reshape(P, DB * P).astype(f)}


class Blk:

    def __init__(self, c, half=0):
        self.c, self.half = c, half

    def __add__(self, j):
        return Blk(self.c + j, self.half)

    @property
    def n(self):
        return self.c + 2 * self.half

    @property
    def slot(self):
        return self.c % 2

    @property
    def uses(self):
        return self.c // 2 + 1 + self.half


class Tally:

    def __init__(self, sem):
        self.sem, self.base, self.k = sem, 0, 0

    def mark(self, ins):
        ins.then_inc(self.sem, 1)
        self.k += 1
        return self.base + self.k

    def enter(self, i, per):
        self.before, self.base, self.k = self.base + self.k, self.base + self.k + per * i, 0

    def leave(self, per, trips):
        assert self.k == per, (self.k, per)
        self.base, self.k = self.before + per * trips, 0


N_RET = 4
N_MLP0 = N_RET + 10 * (RH - 1) + 6
N_KVF = N_MLP0 + 32
N_QG = N_KVF + 9
N_OUT = N_QG + 8
N_MLP1 = N_OUT + 4
N_END = N_MLP1 + 32


def program(nc, io):
    ctx = ExitStack()
    with ctx:
        def sem(name):
            return ctx.enter_context(nc.semaphore(name))

        PS = ctx.enter_context(nc.psum_tensor("PS", [P, 8, 512], F32))
        arena_bytes = 212800
        base = (nc.sbuf_base + 31) // 32 * 32
        ctx.enter_context(nc.sbuf_tensor("arena", [P, arena_bytes // 4], F32))

        def place(name, shape, at, dt=F32):
            n = 4
            for s in shape[1:]:
                n *= s
            n = (n + 31) // 32 * 32
            assert at + n <= arena_bytes, (name, at, n)
            return nc.alloc_sbuf_tensor_at(name, shape, dt, offset=base + at), at + n

        X, at = place("X", [P, KT, T], 0)
        WR = []
        WH = []
        WL = []
        for s in range(2):
            t_, at = place(f"w_raw{s}", [P, KT * BW], at)
            WR.append(t_)
        for s in range(2):
            t_, at = place(f"w_hi{s}", [P, KT * BW], at, F32R)
            WH.append(t_)
            t_, at = place(f"w_lo{s}", [P, KT * BW], at, F32R)
            WL.append(t_)
        CK, at = place("c_keep_sb", [P, KEEP_N], at)
        GN, at = place("gains", [P, 5, KT], at)
        GK, at = place("gain_k", [P, 2], at)
        BF, at = place("b_f_sb", [FH, 1], at)
        R0 = at
        XH, at = place("x_hi", [P, KT, T], R0, F32R)
        XL, at = place("x_lo", [P, KT, T], at, F32R)
        R1 = at
        TT, at = place("temps", [P, 2, T], R1)
        TT4 = TT[:].rearrange("p a (b n) -> p (a b) n", b=2)
        RR, at = place("rms", [P, T], at)
        R2 = at

        CR, at = place("c_ret_sb", [P, RET_N], R2)
        Q, at = place("ret_q", [P, 2, T], at)
        K, at = place("ret_k", [P, 2, T], at)
        QD, at = place("ret_q_decayed", [P, 2, T], at)
        V, at = place("ret_v", [P, 5, DV], at)
        G, at = place("ret_gate", [P, 4, T], at)
        O, at = place("ret_o", [P, 4, T], at)
        S, at = place("ret_state", [P, 2, DV], at)
        KS, at = place("sample_k_parts", [96, DB, DK], at, F32R)
        KM, at = place("meta_k_decayed", [W0, DK], at)
        KD, at = place("k_decayed", [P, 4, DK], at)
        AT, at = place("scores_t", [P, 4, P], at)
        AT0, at = place("scores_t_w0", [W0, W0], at)
        Y0 = at
        YH, at = place("y_hi", [P, 4, T], Y0, F32R)
        YL, at = place("y_lo", [P, 4, T], at, F32R)
        SB = []
        at = Y0
        for s in range(4):
            t_, at = place(f"sample_state{s}", [P, 2, DV], at)
            SB.append(t_)
        VS, _ = place("sample_v_parts", [96, 2, DV], Y0 + 2 * 4 * 4 * T, F32R)
        XT, _ = place("x_tokens", [P, 5, D], R2 + 12000)

        HH, at = place("hidden_hi", [P, KT, T], R2, F32R)
        HL, at = place("hidden_lo", [P, KT, T], at, F32R)
        HT, at = place("hidden_tmp", [P, 2, 2, HF], at)

        KTT, at = place("fox_k_t", [P, KT, T], R2)
        GG, at = place("fox_gate", [P, KT, T], at)
        VV0 = at
        VV, at = place("fox_v", [P, 5, D], at)
        TOK0 = at
        TOK, at = place("fox_tok", [P, 5, D], TOK0)
        LF0 = at
        LF, at = place("logf", [FH, T], LF0)
        CU, at = place("cum_parts", [P, NKEY], at, F32R)
        CF, at = place("c_fox_sb", [P, FOX_N], at)
        NS0 = at
        NS, at = place("c_row_sb", [P, ROW_N], NS0)
        NSR, _ = place("negsel_r", [P, FH * P], NS0, F32R)
        LS, at = place("sample_logf", [P, NSAMP], at)
        LFO, at = place("logf_tok", [P, 5, FH], at)
        GKB, at = place("gain_k_row", [P, DH], at)
        NM, at = place("neg_max", [P, 4], at)
        SM, at = place("row_sum", [P, 4], at)
        RM, at = place("row_inv", [P, 4], at)
        SS, at = place("sum_squares", [P, 5, FH], at)
        PT1, at = place("page_table_row", [1, DB * NPAGE], at, I32)
        PT2, at = place("page_table_col", [DB * NPAGE, 1], at, I32)
        QT, at = place("fox_q_t", [P, KT, T], R0)
        KR0 = at
        PTS, at = place("probs_t", [P, 2, 4 * P], TOK0 + 12288)
        PP0, at = place("probs0", [P, NKEY], at)
        PTM, at = place("probs_t_meta", [P, 2, P], at)
        PP1, _ = place("probs1", [P, NKEY], LF0)
        PP2, _ = place("probs2", [P, NKEY], TOK0 + 8192)
        PP3, _ = place("probs3", [P, NKEY], KR0 + 3 * 4 * D)
        PP = [[PP0, PP1], [PP2, PP3]]
        QZ = [place(f"q_by_head{i}", [P, 2, NPROMPT], TOK0 + 8 * NPROMPT * i)[0] for i in range(2)]
        KR = []
        at = KR0
        for s in range(NKS):
            if s < 3:
                t_, at = place(f"k_page{s}", [P, D], at)
            else:
                t_, _ = place(f"k_page{s}", [P, D], VV0 + 4 * D * (s - 2))
            KR.append(t_)
        QB, at = place("q_blocks", [P, 2, 4, 64], at + 4 * NKEY)
        assert at <= R1
        VR = []
        at = TOK0
        for s in range(NVS):
            if s < 3:
                t_, at = place(f"v_page{s}", [P, D], at)
            else:
                t_, _ = place(f"v_page{s}", [P, D], VV0 + 4 * D * s)
            VR.append(t_)
        KP = []
        for s in range(2):
            t_, at = place(f"k_page_t{s}", [P, KT, P], at)
            KP.append(t_)
        PB, at = place("sample_probs", [P, SK], NS0)
        SEL, at = place("c_selb_sb", [P, DB, P], at)
        PSM, _ = place("sample_probs_t", [P, 8, P], LF0)
        CL, at = place("sample_cum", [P, SK], R1)
        PSN, at = place("sample_probs_t_new", [NSAMP, P], at)
        OX, at = place("o_by_head", [P, 4, DH], at)
        OS, at = place("o_tok", [P, DH], at)
        assert at <= R2
        LFP, _ = place("logf_pages", [DB * NPAGE, PAGE * FH], KR0)
        LFK, _ = place("logf_keys", [P, NPAGE, DB, FH], TOK0)
        YO, _ = place("y_tokens", [P, 5, D], R0)

        def ck(name, rows=P):
            a, n = KEEP[name]
            return CK[0:rows, a:a + n]

        def cf(name):
            a, n = FOX[name]
            return CF[:, a:a + n]

        def cr(name):
            a, n = RET[name]
            return CR[:, a:a + n]

        ident = ck("ident")

        ident_in = sem("ident_in")
        const_in = sem("const_in")
        x_tok_in = sem("x_tok_in")
        x_turned = sem("x_turned")
        x_built = sem("x_built")
        raw_in = [sem("raw_in0"), sem("raw_in1")]
        hi_done = sem("hi_done")
        lo_done = sem("lo_done")
        unit_ready = sem("unit_ready")
        evac_done = sem("evac_done")
        dve_step = sem("dve_step")
        sq_done = sem("sq_done")
        sq_used = sem("sq_used")
        sums_ready = sem("sums_ready")
        root_done = sem("root_done")
        xn_done = sem("xn_done")
        xhi_done = sem("xhi_done")
        xlo_done = sem("xlo_done")
        rot_done = sem("rot_done")
        sig_done = sem("sig_done")
        at_ready = sem("at_ready")
        at_done = sem("at_done")
        kt_ready = sem("kt_ready")
        kd_done = sem("kd_done")
        km_done = sem("km_done")
        vs_high = sem("vs_high")
        vs_done = sem("vs_done")
        ks_high = sem("ks_high")
        ks_copied = sem("ks_copied")
        ks_done = sem("ks_done")
        upd_ready = sem("upd_ready")
        s_done = sem("s_done")
        s_stored = sem("s_stored")
        o_ready = sem("o_ready")
        o_evac = sem("o_evac")
        sb_in = [sem(f"sb_in{s}") for s in range(4)]
        supd_ready = sem("supd_ready")
        sb_done = sem("sb_done")
        cross_ready = sem("cross_ready")
        ot_copied = sem("ot_copied")
        sb_stored = [sem(f"sb_stored{s}") for s in range(4)]
        osq_done = sem("osq_done")
        osq_used = sem("osq_used")
        oroot_done = sem("oroot_done")
        y_done = sem("y_done")
        yhi_done = sem("yhi_done")
        ylo_done = sem("ylo_done")
        sqh_done = sem("sqh_done")
        hhi_done = sem("hhi_done")
        hlo_done = sem("hlo_done")
        y_out = sem("y_out")
        fox_in = sem("fox_in")
        f_neg = sem("f_neg")
        f_exp = sem("f_exp")
        f_ln = sem("f_ln")
        lf_done = sem("lf_done")
        sqt_done = sem("sqt_done")
        sqt_used = sem("sqt_used")
        hroot_done = sem("hroot_done")
        tok_done = sem("tok_done")
        small_ready = sem("small_ready")
        small_done = sem("small_done")
        tok_turned = sem("tok_turned")
        tok_evac = sem("tok_evac")
        out_stored = sem("out_stored")
        k_stored = sem("k_stored")
        gate_done = sem("gate_done")
        logf_in = sem("logf_in")
        lfk_ready = sem("lfk_ready")
        lfk_done = sem("lfk_done")
        lfc_ready = sem("lfc_ready")
        lfc_done = sem("lfc_done")
        rounded = sem("rounded")
        qz_zero = sem("qz_zero")
        qz_done = sem("qz_done")
        s_ready = sem("s_ready")
        masked = sem("masked")
        mx_done = sem("mx_done")
        ex_done = sem("ex_done")
        inv_row = sem("inv_row")
        pn_done = sem("pn_done")
        pt_ready = sem("pt_ready")
        pt_evac = sem("pt_evac")
        pv_ready = sem("pv_ready")
        pv_evac = sem("pv_evac")
        k_in = [sem(f"k_in{s}") for s in range(NKS)]
        v_in = [sem(f"v_in{s}") for s in range(NVS)]
        k_used = sem("k_used")
        kp_evac = sem("kp_evac")
        sc_used = sem("sc_used")
        v_used = sem("v_used")
        qb_done = sem("qb_done")
        ss_ready = sem("ss_ready")
        smx_done = sem("smx_done")
        sex_done = sem("sex_done")
        spt_ready = sem("spt_ready")
        spv_ready = sem("spv_ready")
        os_done = sem("os_done")
        ot_ready = sem("ot_ready")
        ot_done = sem("ot_done")
        sel_in = sem("sel_in")
        fyhi_done = sem("fyhi_done")
        fylo_done = sem("fylo_done")
        yo_ready = sem("yo_ready")
        yo_done = sem("yo_done")

        w_in = io["w_ret_in"].rearrange("a (t p) n -> p (a t) n", p=P)
        w_ro = io["w_ret_out"].rearrange("a (h t p) n -> p (a h) t n", p=P, t=DV // P)
        w_up = [io["w_mlp_up"][l].rearrange("(t p) n -> p t n", p=P) for l in range(2)]
        w_dn = [io["w_mlp_down"][l].rearrange("(c t p) n -> p c t n", p=P, t=KT) for l in range(2)]

        w_kvf = io["w_kvf"].rearrange("(t p) n -> p t n", p=P)
        w_qg = io["w_fox_qg"].rearrange("a (t p) n -> p (a t) n", p=P)
        w_fo = io["w_fox_out"].rearrange("a (t p) n -> p (a t) n", p=P)
        k_pool = io["cache_k"].rearrange("n k h d -> n k (h d)")
        v_pool = io["cache_v"].rearrange("n k h d -> n k (h d)")

        def keys_of(qb):
            return NMETA + P * (qb + 1)

        def norm_full(k):
            return [0, 1, 2, None, 3][k]

        def score_cols(j, par):
            b = [par, 2 + par, par, 2 + 2 * par][j % 4]
            return PS[:, b:b + 2, :].rearrange("p a n -> p (a n)")[:, 0:keys_of(j % 4)]

        def out_banks(j):
            return (1, 1) if j % 4 == 2 else (4, 5)

        def scores_first(j):
            return j % 4 in (0, 3)

        def turn_no(b, what):
            if b == 0:
                return what
            order = [0, 1, "probs", 2, 3, "new", 4, 5, 6, 7] if b < DB else ["probs", "new"]
            return NPAGE + 10 * (b - 1) + order.index(what)

        def turn_bank(b, what):
            return 4 + 2 * (turn_no(b, what) % 2)

        block = ctx.enter_context(nc.Block())

        @block.sync
        def _(sp):
            def weights(n, src, kt=KT, cols=BW):
                sp.wait_ge(lo_done, n.n + 1)
                sp.dma_start(WR[n.slot][:, 0:kt * cols].rearrange("p (t n) -> p t n", t=kt), src) \
                    .then_inc(raw_in[n.slot], 16)

            def qkv(n, h, js=range(4)):
                for j in js:
                    col = [DK * h, RH * DK + DK * h, 2 * RH * DK + DV * h, 2 * RH * DK + DV * h + BW][j]
                    weights(n + j, w_in[:, :, bass.ds(col, BW)])

            def gate(n, h):
                for j in range(2):
                    weights(n + j, w_in[:, :, bass.ds(2 * RH * DK + RH * DV + DV * h + BW * j, BW)])

            def ret_out(n, h, js=range(4)):
                for j in js:
                    weights(n + j, w_ro[:, bass.ds(h, 1), :, BW * j:BW * j + BW].rearrange("p o t n -> p (o t) n"),
                            kt=DV // P)

            def states(h):
                for b in range(DB):
                    if b < 4:
                        sp.wait_ge(unit_ready, 10 * h + 6)
                    else:
                        sp.wait_ge(sb_stored[b % 4], 32 * h + 16)
                    sp.dma_start(SB[b % 4][:], io["state_ret"][0, b, bass.ds(h, 1)]
                                 .rearrange("o (t p) e -> p (o t) e", p=P)).then_inc(sb_in[b % 4], 16)

            sp.dma_start(CK[:], io["c_keep"]).then_inc(ident_in, 16)
            sp.dma_start(XT[0:NSAMP, 0, :], io["x_sample"].rearrange("b s d -> (b s) d")).then_inc(x_tok_in, 16)
            sp.dma_start(XT[NSAMP:W0, 0, :], io["meta"]).then_inc(x_tok_in, 16)
            sp.dma_start(XT[:, 1:5, :], io["x_prompt"].rearrange("o (c p) d -> p (o c) d", p=P)) \
                .then_inc(x_tok_in, 16)
            with nc.allow_non_contiguous_dma(reason="the gains, a few KB"):
                for k, g in enumerate((io["g_attn"][0:1], io["g_mlp"][0:1], io["g_kv"].rearrange("(o d) -> o d", o=1),
                                       io["g_attn"][1:2], io["g_mlp"][1:2])):
                    sp.dma_start(GN[:, k, :], g.rearrange("o (t p) -> p (o t)", p=P)).then_inc(const_in, 16)
                for half in range(2):
                    rows = slice(DH * half, DH * half + DH)
                    sp.dma_start(GK[rows, 0:1], io["g_k"].rearrange("(p o) -> p o", o=1)).then_inc(const_in, 16)
                    sp.dma_start(GK[rows, 1:2], io["g_q"].rearrange("o p -> p o")).then_inc(const_in, 16)
                sp.dma_start(BF[:], io["b_f"].rearrange("(p o) -> p o", o=1)).then_inc(const_in, 16)
            sp.dma_start(CR[:], io["c_ret"]).then_inc(const_in, 16)
            qkv(Blk(0), 0)
            with sp.Fori(0, RH - 1) as h:
                n = Blk(N_RET, 5 * h)
                gate(n, h)
                qkv(n + 2, h + 1, (0, 1))
                states(h)
                qkv(n + 2, h + 1, (2, 3))
                ret_out(n + 6, h)
            h, n = RH - 1, Blk(N_RET + 10 * (RH - 1))
            gate(n, h)
            states(h)
            ret_out(n + 2, h)

            def mlp(n0, l):
                with sp.Fori(0, 4) as c:
                    n = Blk(n0, 4 * c)
                    for j in range(4):
                        weights(n + j, w_up[l][:, :, bass.ds(D * c + BW * j, BW)])
                    for j in range(4):
                        weights(n + 4 + j, w_dn[l][:, bass.ds(c, 1), :, BW * j:BW * j + BW]
                                .rearrange("p o t n -> p (o t) n"))
            mlp(N_MLP0, 0)

            n = Blk(N_KVF)
            sp.wait_ge(lo_done, n.n + 1)
            sp.dma_start(WR[n.slot][:].rearrange("p (t n) -> p t n", t=KT)[:, :, 0:FH], w_kvf[:, :, 2 * D:2 * D + FH]) \
                .then_inc(raw_in[n.slot], 16)
            weights(Blk(N_KVF + 1), w_kvf[:, :, 0:BW])
            sp.wait_ge(unit_ready, N_KVF + 2)
            sp.dma_start(CF[:], io["c_fox"]).then_inc(fox_in, 16)
            sp.dma_start(NS[:], io["c_row"]).then_inc(fox_in, 16)
            with nc.allow_non_contiguous_dma(reason="the gain of the keys, on every partition"):
                sp.dma_start(GKB[:], io["g_k"].rearrange("(o d) -> o d", o=1).to_broadcast([P, DH])) \
                    .then_inc(fox_in, 16)
            sp.dma_start(PT1[:], io["page_table"].rearrange("(o b) p -> o (b p)", o=1)).then_inc(fox_in, 16)
            sp.dma_start(PT2[:], io["page_table"].rearrange("b (p o) -> (b p) o", o=1)).then_inc(fox_in, 16)
            with sp.Fori(0, 3) as i:
                weights(Blk(N_KVF + 2, i), w_kvf[:, :, bass.ds(2 * BW * i + BW, BW)])
                weights(Blk(N_KVF + 3, i), w_kvf[:, :, bass.ds(2 * BW * i + 2 * BW, BW)])
            weights(Blk(N_KVF + 8), w_kvf[:, :, 7 * BW:8 * BW])
            with sp.Fori(0, 4) as i:
                weights(Blk(N_QG, i), w_qg[:, :, bass.ds(2 * BW * i, BW)])
                weights(Blk(N_QG + 1, i), w_qg[:, :, bass.ds(2 * BW * i + BW, BW)])
            for j in range(2):
                weights(Blk(N_OUT + j), w_fo[:, :, BW * j:BW * j + BW])
            sp.wait_ge(mx_done, 64)
            sp.dma_start(SEL[:], io["c_selb"].rearrange("p (b n) -> p b n", b=DB)).then_inc(sel_in, 16)
            sp.wait_ge(lfc_done, 2)
            sp.wait_ge(fox_in, 16 * 5)

            def k_page(kn):
                if kn == 3:
                    sp.wait_ge(pv_ready, 32)
                    sp.wait_ge(out_stored, 16 * 6)
                if kn >= NKS:
                    sp.wait_ge(k_used, kn - NKS + 1)
                page = sp.value_load(PT1[0:1, kn:kn + 1], min_val=0, max_val=io["cache_k"].shape[0] - 1)
                sp.dma_start(KR[kn % NKS][:], k_pool[bass.ds(page, 1)].rearrange("o k f -> k (o f)")) \
                    .then_inc(k_in[kn % NKS], 16)

            def v_page(vn):
                if vn >= NVS:
                    sp.wait_ge(v_used, vn - NVS + 1)
                page = sp.value_load(PT1[0:1, vn:vn + 1], min_val=0, max_val=io["cache_v"].shape[0] - 1)
                sp.dma_start(VR[vn % NVS][:], v_pool[bass.ds(page, 1)].rearrange("o k f -> k (o f)")) \
                    .then_inc(v_in[vn % NVS], 16)

            for b in range(DB + 1):
                for p in range(4 if b < DB else 0):
                    k_page(NPAGE * b + p)
                for i in range(4):
                    for p in range(2 * i if b else 0, 2 * i + 2 if b else 0):
                        v_page(NPAGE * (b - 1) + p)
                    if b < DB:
                        k_page(NPAGE * b + 4 + i)
            for j in range(2, 4):
                weights(Blk(N_OUT + j), w_fo[:, :, BW * j:BW * j + BW])
            mlp(N_MLP1, 1)
            for w in range(5):
                sp.wait_ge(yo_done, 2 * (w + 1))
                if w == 0:
                    sp.dma_start(io["y_sample"].rearrange("b s d -> (b s) d"), YO[0:NSAMP, 0, :]).then_inc(y_out, 16)
                else:
                    sp.dma_start(io["y_prompt"][0, P * (w - 1):P * w, :], YO[:, w, :]).then_inc(y_out, 16)
            sp.wait_ge(y_out, 16 * 5)

        @block.gpsimd
        def _(pool):
            pool.sem_inc(lo_done, 2)

            def split(n):
                pool.wait_ge(hi_done, n.n + 1)
                pool.tensor_tensor(WL[n.slot][:], WR[n.slot][:], WH[n.slot][:].bitcast(F32), ALU.subtract) \
                    .then_inc(lo_done, 1)

            with pool.Fori(0, (N_OUT + 1) // 2) as i:
                split(Blk(0, i))
                split(Blk(1, i))
            split(Blk(N_OUT + 1))
            pool.wait_ge(fox_in, 16 * 5)
            pool.wait_ge(unit_ready, N_OUT + 2)
            pool.indirect_dma_start(LFP[:], None, io["cache_logf"].rearrange("n k h -> n (k h)"),
                                    bass.IndirectOffsetOnAxis(ap=PT2[:, 0:1], axis=0)).then_inc(logf_in, 16)
            pool.wait_ge(lfc_ready, 1)
            for i in range(2):
                pool.memset(QZ[i][:], 0.0).then_inc(qz_zero, 1)
            with pool.Fori(0, (N_END - N_OUT - 2) // 2) as i:
                split(Blk(N_OUT + 2, i))
                split(Blk(N_OUT + 3, i))

        @block.tensor
        def _(pe):
            pe.sem_inc(unit_ready, 2)

            def bank(n, m, hf):
                return PS[:, 4 * n.slot + 2 * m + hf, 0:HF]

            def begin(n):
                pe.wait_ge(lo_done, n.n + 3)
                pe.wait_ge(evac_done, n.n + 1)

            def unit(n, xh, xl, kt=KT, tile=None):
                begin(n)
                wh, wl = WH[n.slot], WL[n.slot]
                for t in range(kt):
                    if tile:
                        tile(t)
                    for m in range(2):
                        for hf in range(2):
                            cols = slice(HF * hf, HF * hf + HF)
                            w = slice(BW * t + P * m, BW * t + P * m + P)
                            o = bank(n, m, hf)
                            pe.matmul(o, wh[:, w], xh[:, t, cols], start=(t == 0), stop=False)
                            pe.matmul(o, wh[:, w], xl[:, t, cols], start=False, stop=False)
                            last = pe.matmul(o, wl[:, w], xh[:, t, cols], start=False, stop=(t == kt - 1))
                last.then_inc(unit_ready, 1)

            def turn(src, first):
                for t in range(KT):
                    if t >= 4:
                        pe.wait_ge(tok_evac, first + t - 3)
                    for w, (a, n) in enumerate(WINDOWS):
                        o = PS[:, 2 * (t % 4), a:a + n] if w < 4 else PS[:, 2 * (t % 4) + 1, 0:P]
                        last = pe.transpose(o, src[0:n, w, P * t:P * t + P], ident[0:n, 0:n])
                    last.then_inc(tok_turned, 1)
                pe.wait_ge(tok_evac, first + KT)

            def unit_tok(n, tile=None):
                begin(n)
                wh, wl = WH[n.slot], WL[n.slot]

                def products(w, t, start):
                    a = WINDOWS[w][0]
                    tok = slice(a, a + P)
                    o = PS[:, 4 * n.slot + w // 2, BW * (w % 2):BW * (w % 2) + BW]
                    c = slice(BW * t, BW * t + BW)
                    skip = tile is not None
                    pe.matmul(o, XH[:, t, tok], wh[:, c], start=start, stop=False, skip_group_check=skip)
                    pe.matmul(o, XL[:, t, tok], wh[:, c], start=False, stop=False, skip_group_check=skip)
                    return pe.matmul(o, XH[:, t, tok], wl[:, c], start=False, stop=(t == KT - 1),
                                     skip_group_check=skip)

                if tile:
                    for t in range(KT):
                        tile(t)
                        for w in range(5):
                            last = products(w, t, t == 0 and w % 2 == 0)
                else:
                    for w in range(5):
                        for t in range(KT):
                            last = products(w, t, t == 0)
                last.then_inc(unit_ready, 1)

            def norm_sum(k, n):
                pe.wait_ge(evac_done, n + 2)
                pe.wait_ge(sq_used, KT * (norm_full(k) + 1))
                for hf in range(2):
                    last = pe.matmul(PS[:, hf, 0:HF], ck("ones"), RR[:, HF * hf:HF * hf + HF], start=True, stop=True)
                last.then_inc(sums_ready, 1)

            def normed(k):
                return lambda t: pe.wait_ge(xlo_done, KT * k + t + 1)

            pe.wait_ge(ident_in, 16)
            pe.wait_ge(x_tok_in, 48)
            for t in range(KT):
                if t >= 4:
                    pe.wait_ge(x_built, t - 3)
                for w, (a, n) in enumerate(WINDOWS):
                    o = PS[:, 2 * (t % 4), a:a + n] if w < 4 else PS[:, 2 * (t % 4) + 1, 0:P]
                    last = pe.transpose(o, XT[0:n, w, P * t:P * t + P], ident[0:n, 0:n])
                last.then_inc(x_turned, 1)
            pe.wait_ge(x_built, KT)

            def qkv(n, tile=None, h=None):
                unit(n, XH, XL, tile=tile)
                if h is not None:
                    high_banks(h)
                unit(n + 1, XH, XL)
                unit_tok(n + 2)
                unit_tok(n + 3)

            def sample_states(g, h):
                for i in range(4):
                    pe.wait_ge(sb_in[i], 32 * h + 16 * (g + 1))
                for d in range(2):
                    for i in range(4):
                        last = pe.matmul(PS[32 * i:32 * i + 32, [5, 3][g], :], QD[:, d, 32 * g:32 * g + 32],
                                         SB[i][:, d, :], start=(d == 0), stop=(d == 1))
                last.then_inc(cross_ready, 1)

            def own_queries(g, h):
                pe.wait_ge(ot_copied, 2 * h + g + 1)
                for v in range(4):
                    o = W0 * v + 32 * g
                    last = pe.matmul(PS[:, 2, o:o + 32], RR[:, P * v:P * v + P], cr("own_q"), start=False,
                                     stop=True, skip_group_check=True)
                return last

            def high_banks(h):
                pe.wait_ge(sb_done, 8 * h + 8)
                pe.wait_ge(oroot_done, 2 * h + 1)

            def sum_squares(hf, h):
                pe.wait_ge(osq_done, 2 * h + 2 - hf)
                pe.wait_ge(o_evac, 5 * h + 4)
                for v in range(4):
                    last = pe.matmul(PS[:, 4 + hf, 0:HF], ck("ones"), TT4[:, v, :], start=(v == 0), stop=(v == 3))
                last.then_inc(osq_used, 1)

            def state_update(b, bk, h):
                if b % 4 == 0:
                    pe.wait_ge(vs_done, 2 * h + 2)
                    pe.wait_ge(ks_copied, 2 * h + b // 4 + 1)
                    pe.wait_ge(ks_done, 2 * h + b // 4 + 1)
                before = [None, 0, 1, 2, 3, None, 4, 5][b]
                if before is not None:
                    pe.wait_ge(sb_done, 8 * h + before + 1)
                for d in range(2):
                    last = pe.matmul(PS[:, bk + d, :], KS[:, b, P * d:P * d + P], VS[:, b // 4, :], start=True,
                                     stop=True)
                last.then_inc(supd_ready, 1)

            def retention(n, h, last_head=False):
                if not last_head:
                    unit(n, XH, XL)
                    unit(n + 1, XH, XL)
                gates = 0 if last_head else 2
                pe.wait_ge(evac_done, n.n + gates + 1)
                pe.wait_ge(rot_done, 2 * h + 2)
                for c in range(4):
                    a = W0 + P * c
                    for d in range(2):
                        pe.matmul(PS[:, 0, P * c:P * c + P], K[:, d, a:a + P], Q[:, d, a:a + P],
                                  start=(d == 0), stop=(d == 1))
                for d in range(2):
                    last = pe.matmul(PS[0:W0, 1, 0:W0], K[:, d, 0:W0], Q[:, d, 0:W0], start=(d == 0), stop=(d == 1))
                last.then_inc(at_ready, 1)
                for c in range(4):
                    a = W0 + P * c
                    for d in range(2):
                        o = DK * (c % 2) + P * d
                        pe.transpose(PS[:, 2 + c // 2, o:o + P], K[:, d, a:a + P], ident)
                pe.wait_ge(evac_done, n.n + gates + 2)
                for d in range(2):
                    last = pe.transpose(PS[0:W0, 4, P * d:P * d + P], K[:, d, 0:W0], ident)
                last.then_inc(kt_ready, 1)
                sample_states(0, h)
                pe.wait_ge(km_done, h + 1)
                for d in range(2):
                    last = pe.matmul(PS[:, 6 + d, :], KM[:, P * d:P * d + P], V[0:W0, 0, :], start=True, stop=True)
                last.then_inc(upd_ready, 1)
                pe.wait_ge(at_done, h + 1)
                pe.wait_ge(kd_done, h + 1)
                pe.wait_ge(ot_copied, 2 * h + 1)
                for c in range(1, 5):
                    a = W0 + P * (c - 1)
                    ob = 4 + c % 2
                    if c > 2:
                        pe.wait_ge(o_evac, 5 * h + c - 2)
                    if c == 2:
                        pe.wait_ge(ks_done, 2 * h + 2)
                    for v in range(4):
                        pe.matmul(PS[:, ob, P * v:P * v + P], V[:, c, P * v:P * v + P], AT[:, c - 1, :],
                                  start=(v == 0), stop=False, skip_group_check=True)
                    pe.wait_ge(s_done, 5 * h + c)
                    for v in range(4):
                        for d in range(2):
                            last = pe.matmul(PS[:, ob, P * v:P * v + P], S[:, d, P * v:P * v + P], QD[:, d, a:a + P],
                                             start=False, stop=(d == 1), skip_group_check=True)
                    last.then_inc(o_ready, 1)
                    if c in (2, 3):
                        state_update(2 * c - 3, 0, h)
                    for d in range(2):
                        last = pe.matmul(PS[:, 6 + d, :], KD[:, c - 1, P * d:P * d + P], V[:, c, :],
                                         start=True, stop=True)
                    last.then_inc(upd_ready, 1)
                    if c < 3:
                        state_update(2 * c - 2, 0, h)
                for v in range(4):
                    pe.matmul(PS[:, 2, W0 * v:W0 * v + W0], V[0:W0, 0, P * v:P * v + P], AT0[:],
                              start=(v == 0), stop=False, skip_group_check=True)
                own_queries(0, h)
                sum_squares(1, h)
                sample_states(1, h)
                state_update(4, 0, h)
                own_queries(1, h).then_inc(o_ready, 1)
                pe.wait_ge(s_done, 5 * h + 5)
                state_update(5, 6, h)
                state_update(6, 0, h)
                state_update(7, 6, h)
                sum_squares(0, h)
                pe.wait_ge(sb_done, 8 * h + 7)
                pe.wait_ge(o_evac, 5 * h + 5)
                if last_head:
                    unit(n, XH, XL)
                    high_banks(h)
                    unit(n + 1, XH, XL)

            def ret_out(n, h):
                unit(n, YH, YL, kt=DV // P, tile=lambda t: pe.wait_ge(ylo_done, 4 * h + t + 1))
                high_banks(h)
                for j in range(1, 4):
                    unit(n + j, YH, YL, kt=DV // P)

            norm_sum(0, 0)
            qkv(Blk(0), normed(0))
            with pe.Fori(0, RH - 1) as h:
                n = Blk(N_RET, 5 * h)
                retention(n, h)
                qkv(n + 2, h=h)
                ret_out(n + 6, h)
            n = Blk(N_RET + 10 * (RH - 1))
            retention(n, RH - 1, last_head=True)
            ret_out(n + 2, RH - 1)

            def mlp(n0, l):
                with pe.Fori(0, 4) as c:
                    n = Blk(n0, 4 * c)
                    unit(n, XH, XL, tile=normed(4 if l else 1))
                    for j in range(1, 4):
                        unit(n + j, XH, XL)
                    unit(n + 4, HH, HL, tile=lambda t: pe.wait_ge(hlo_done, 16 * l + 4 * c + t // 2 + 1))
                    for j in range(1, 4):
                        unit(n + 4 + j, HH, HL)
            norm_sum(1, N_MLP0)
            mlp(N_MLP0, 0)

            norm_sum(2, N_KVF)
            n = Blk(N_KVF)
            begin(n)
            for t in range(KT):
                normed(2)(t)
                for hf in range(2):
                    cols = slice(HF * hf, HF * hf + HF)
                    w = slice(BW * t, BW * t + P)
                    pe.matmul(bank(n, 0, hf), WH[n.slot][:, w], XH[:, t, cols], start=(t == 0), stop=False)
                    pe.matmul(bank(n, 0, hf), WH[n.slot][:, w], XL[:, t, cols], start=False, stop=False)
                    last = pe.matmul(bank(n, 0, hf), WL[n.slot][:, w], XH[:, t, cols], start=False, stop=(t == KT - 1))
            last.then_inc(unit_ready, 1)
            with pe.Fori(0, 4) as i:
                unit_tok(Blk(N_KVF + 1, i))
                unit_tok(Blk(N_KVF + 2, i))
            pe.wait_ge(fox_in, 16 * 5)
            pe.wait_ge(evac_done, N_QG + 2)
            pe.wait_ge(lf_done, 2)
            for w, (a, n) in enumerate(WINDOWS):
                pe.transpose(PS[0:n, 0, FH * w:FH * w + FH], LF[:, a:a + n], ident[0:FH, 0:FH])
            a, n = ROW["rep"]
            pe.matmul(PS[:, 1, 0:NSAMP], NS[0:FH, a:a + n], LF[:, 0:NSAMP], start=True, stop=True) \
                .then_inc(small_ready, 1)
            pe.wait_ge(small_done, 1)
            pe.wait_ge(tok_done, 5)
            turn(TOK, 0)
            unit_tok(Blk(N_QG), normed(3))
            for j in range(1, 4):
                unit_tok(Blk(N_QG + j))
            with pe.Fori(0, 2) as i:
                unit(Blk(N_QG + 4, i), XH, XL)
                unit(Blk(N_QG + 5, i), XH, XL)
            pe.wait_ge(evac_done, N_OUT + 2)
            pe.wait_ge(tok_done, 10)
            turn(TOK, KT)

            pe.wait_ge(logf_in, 16)
            for h in range(FH):
                last = pe.transpose(PS[:, h // 8, 64 * (h % 8):64 * (h % 8) + 64],
                                    LFP[:].rearrange("q (k h) -> q k h", h=FH)[:, :, h], ident[0:64, 0:64])
            last.then_inc(lfk_ready, 1)
            pe.wait_ge(lfk_done, 2)
            for p in range(NPAGE):
                last = pe.transpose(PS[:, 2 + p // 4, P * (p % 4):P * (p % 4) + P],
                                    LFK[:, p].rearrange("k b h -> k (b h)"), ident)
            last.then_inc(lfc_ready, 1)
            pe.wait_ge(lfc_done, 2)

            def scores(j, par):
                t, n = j // 4, keys_of(j % 4)
                pieces = [(a, min(a + 512, n)) for a in range(0, n, 512)]
                if j % 4 == 0:
                    pe.wait_ge(qz_done, t + 1)
                for a, e in pieces:
                    pe.matmul(score_cols(j, par)[:, a:e], NSR[:, P * (2 * t + par):P * (2 * t + par) + P], CU[:, a:e],
                              start=True, stop=False)
                for a, e in pieces:
                    last = pe.matmul(score_cols(j, par)[:, a:e], QZ[t % 2][:, par, P * (j % 4):P * (j % 4) + P],
                                     KTT[:, t, NSAMP + a:NSAMP + e], start=False, stop=True)
                last.then_inc(s_ready, 1)

            def probs_t(j):
                for par in range(2):
                    pe.wait_ge(pn_done, 2 * j + par + 1)
                    for kb in range(j % 4 + 1):
                        pe.transpose(PS[:, 6 + par, P * kb:P * kb + P],
                                     PP[j % 2][par][:, NMETA + P * kb:NMETA + P * kb + P], ident)
                for par in range(2):
                    last = pe.transpose(PS[0:NMETA, out_banks(j)[0], P * par:P * par + P],
                                        PP[j % 2][par][:, 0:NMETA], ident)
                last.then_inc(pt_ready, 1)

            def values(j):
                t, qb = j // 4, j % 4
                pe.wait_ge(pt_evac, 2 * j + 2)
                if j:
                    pe.wait_ge(pv_evac, j)
                for par in range(2):
                    h = slice(DH * (2 * t + par), DH * (2 * t + par) + DH)
                    o = PS[DH * par:DH * par + DH, out_banks(j)[1], 256:384]
                    pe.matmul(o, VV[NSAMP:W0, 0, h], PTM[NSAMP:W0, par, :], start=True, stop=False)
                    for kb in range(qb + 1):
                        last = pe.matmul(o, VV[:, 1 + kb, h], PTS[:, par, P * kb:P * kb + P], start=False,
                                         stop=(kb == qb))
                last.then_inc(pv_ready, 1)

            NPAIR = 4 * KT
            pe.wait_ge(rounded, 1)
            for j in range(2):
                for par in range(2):
                    scores(j, par)
            for j in range(NPAIR):
                probs_t(j)
                if j + 2 < NPAIR:
                    scores(j + 2, 0)
                    if scores_first(j):
                        scores(j + 2, 1)
                values(j)
                if j + 2 < NPAIR and not scores_first(j):
                    pe.wait_ge(pv_evac, j + 1)
                    scores(j + 2, 1)
            pe.wait_ge(pv_evac, NPAIR)

            def slot_begin(b, what):
                k = turn_no(b, what)
                if k >= 2:
                    pe.wait_ge(kp_evac, k - 1)
                return turn_bank(b, what)

            def page_t(b, p):
                kn = NPAGE * b + p
                pe.wait_ge(k_in[kn % NKS], 16 * (kn // NKS + 1))
                s = slot_begin(b, p)
                for t in range(KT):
                    last = pe.transpose(PS[:, s + t // 4, P * (t % 4):P * (t % 4) + P],
                                        KR[kn % NKS][:, P * t:P * t + P], ident)
                last.then_inc(k_used, 1)

            def bias(b):
                if b == 0:
                    pe.wait_ge(sel_in, 16)
                else:
                    pe.wait_ge(sex_done, b)
                for i, (a, e) in enumerate(((0, 512), (512, 1024), (1024, SK))):
                    pe.matmul(PS[:, i, 0:e - a], SEL[:, b, :], CL[:, a:e], start=True, stop=False,
                              skip_group_check=True)

            def q_k(b, o_bank, o_cols, rhs, stop=True):
                for e in range(2):
                    for g in range(4):
                        last = pe.matmul(PS[32 * g:32 * g + 32, o_bank, o_cols], QB[:, b % 2, g, 32 * e:32 * e + 32],
                                         rhs(2 * g + e), start=False, stop=(e == 1), skip_group_check=True)
                return last

            def page_scores(b, p):
                kn = NPAGE * b + p
                pe.wait_ge(kp_evac, turn_no(b, p) + 1)
                if p == 0:
                    pe.wait_ge(qb_done, b + 1)
                q_k(b, p // 4, slice(P * (p % 4), P * (p % 4) + P), lambda t: KP[kn % 2][:, t, :]).then_inc(sc_used, 1)

            def probs_t_s(b):
                pe.wait_ge(sex_done, b + 1)
                s = slot_begin(b + 1, "probs")
                for p in range(NPAGE):
                    last = pe.transpose(PS[:, s + p // 4, P * (p % 4):P * (p % 4) + P], PB[:, P * p:P * p + P], ident)
                last.then_inc(spt_ready, 1)

            def probs_t_new(b):
                pe.transpose(PS[0:NSAMP, slot_begin(b + 1, "new"), 0:P], PB[:, PAST:SK], ident).then_inc(spt_ready, 1)

            def begin_values(b):
                pe.wait_ge(kp_evac, turn_no(b + 1, "new") + 1)
                if b > 0:
                    pe.wait_ge(ot_done, 2 * b)

            def page_values(b, p):
                vn = NPAGE * b + p
                pe.wait_ge(v_in[vn % NVS], 16 * (vn // NVS + 1))
                for g in range(4):
                    last = pe.matmul(PS[32 * g:32 * g + 32, 3, 0:256], PSM[:, p, 32 * g:32 * g + 32],
                                     VR[vn % NVS][:, 256 * g:256 * g + 256], start=(p == 0), stop=False)
                last.then_inc(v_used, 1)

            def new_values(b):
                for g in range(4):
                    last = pe.matmul(PS[32 * g:32 * g + 32, 3, 0:256], PSN[:, 32 * g:32 * g + 32],
                                     VV[0:NSAMP, 0, 256 * g:256 * g + 256], start=False, stop=True)
                last.then_inc(spv_ready, 1)

            def out_t(b):
                pe.wait_ge(os_done, b + 1)
                pe.transpose(PS[0:DH, 3, 256:384], OS[:], ident).then_inc(ot_ready, 1)

            for b in range(DB + 1):
                if b < DB:
                    page_t(b, 0)
                    page_t(b, 1)
                    bias(b)
                    page_scores(b, 0)
                if b > 0:
                    probs_t_s(b - 1)
                if b < DB:
                    page_scores(b, 1)
                    page_t(b, 2)
                    page_t(b, 3)
                    page_scores(b, 2)
                if b > 0:
                    probs_t_new(b - 1)
                if b < DB:
                    page_scores(b, 3)
                if b > 0:
                    begin_values(b - 1)
                for p in range(4, 8):
                    if b > 0:
                        page_values(b - 1, 2 * p - 8)
                        page_values(b - 1, 2 * p - 7)
                    if b < DB:
                        page_t(b, p)
                        if p >= 5:
                            page_scores(b, p - 1)
                if b > 0:
                    new_values(b - 1)
                if b < DB:
                    page_scores(b, 7)
                    q_k(b, 2, slice(0, NSAMP), lambda t: KTT[:, t, 0:NSAMP]).then_inc(ss_ready, 1)
                if b > 0:
                    out_t(b - 1)

            pe.wait_ge(ot_done, 2 * DB)
            unit(Blk(N_OUT), XH, XL, tile=lambda t: pe.wait_ge(fylo_done, t + 1))
            for j in range(1, 4):
                unit(Blk(N_OUT + j), XH, XL)
            norm_sum(4, N_MLP1)
            mlp(N_MLP1, 1)
            pe.wait_ge(evac_done, N_END + 2)
            for w, (a, n) in enumerate(WINDOWS):
                for half in range(2):
                    k = 2 * w + half
                    if k >= 8:
                        pe.wait_ge(yo_done, k - 7)
                    for t in range(4):
                        last = pe.transpose(PS[0:n, k % 8, P * t:P * t + P], X[:, 4 * half + t, a:a + n], ident)
                    last.then_inc(yo_ready, 1)

        @block.scalar
        def _(act):
            def w_hi(n):
                act.wait_ge(raw_in[n.slot], 16 * n.uses)
                act.wait_ge(unit_ready, n.n + 1)
                act.activation(WH[n.slot][:], WR[n.slot][:], ACT.Copy).then_inc(hi_done, 1)

            def inverse_root(sums, width, done, before):
                act.activation(RR[:].rearrange("p (a n) -> p a n", a=2), sums, ACT.Ln, scale=1.0 / width,
                               bias=ck("eps")).then_inc(done, 1)
                act.wait_ge(done, before + 1)
                act.activation(RR[:], RR[:], ACT.Exp, scale=-0.5).then_inc(done, 1)

            def squares(k, t):
                i = KT * norm_full(k) + t
                if i >= 2:
                    act.wait_ge(sq_used, i - 1)
                act.activation(TT[:, t % 2, :], X[:, t, :], ACT.Square).then_inc(sq_done, 1)

            def block_squares(k, n, j):
                act.wait_ge(evac_done, n.n + 3)
                squares(k, 2 * j)
                squares(k, 2 * j + 1)

            def norm(k, n):
                f = norm_full(k)
                if f is not None:
                    act.wait_ge(sums_ready, f + 1)
                    inverse_root(PS[:, 0:2, 0:HF], D, root_done, 2 * f)
                act.wait_ge(unit_ready, n + 2)
                for t in range(KT):
                    act.wait_ge(xn_done, KT * k + t + 1)
                    act.activation(XH[:, t, :], TT[:, t % 2, :], ACT.Copy).then_inc(xhi_done, 1)

            for t in range(KT):
                act.wait_ge(x_turned, t + 1)
                act.activation(X[:, t, 0:T - P], PS[:, 2 * (t % 4), 0:T - P], ACT.Copy)
                act.activation(X[:, t, T - P:T], PS[:, 2 * (t % 4) + 1, 0:P], ACT.Copy).then_inc(x_built, 1)
                act.wait_ge(x_built, t + 1)
                squares(0, t)
            w_hi(Blk(0))
            act.wait_ge(const_in, 16 * 11)
            norm(0, 0)
            w_hi(Blk(1))
            for j in range(4):
                w_hi(Blk(2 + j))

            def gate(n, h, js=range(2)):
                for j in js:
                    m = n + j
                    w_hi(m + 2)
                    act.wait_ge(unit_ready, m.n + 3)
                    for t in range(2):
                        ins = act.activation(G[:, 2 * j + t, :].rearrange("p (a n) -> p a n", a=2),
                                             PS[:, 4 * m.slot + 2 * t:4 * m.slot + 2 * t + 2, 0:HF], ACT.Sigmoid)
                    ins.then_inc(sig_done, 1)

            def retention(n, h, last_head=False):
                act.wait_ge(evac_done, n.n + 2)
                for g, row in ((0, 0), (0, 64), (1, 32), (1, 64)):
                    act.activation(VS[row:row + 32, g, :], V[32 * g:32 * g + 32, 0, :], ACT.Copy).then_inc(vs_high, 1)
                if not last_head:
                    gate(n, h)

                def rows_copy(g):
                    act.wait_ge(cross_ready, 2 * h + g + 1)
                    act.activation(RR[:, 0:DV], PS[:, [5, 3][g], :], ACT.Copy).then_inc(ot_copied, 1)

                def squares(hf):
                    act.activation(TT4, O[:, :, HF * hf:HF * hf + HF], ACT.Square).then_inc(osq_done, 1)

                def states_out(b):
                    act.wait_ge(sb_done, 8 * h + b + 1)
                    act.dma_start(io["state_ret_sample"][0, b, bass.ds(h, 1)]
                                  .rearrange("o (t p) e -> p (o t) e", p=P), SB[b % 4][:]) \
                        .then_inc(sb_stored[b % 4], 16)

                act.wait_ge(kt_ready, h + 1)
                act.activation(KD[:].rearrange("p c d -> p (c d)"), PS[:, 2:4, :].rearrange("p a n -> p (a n)"),
                               ACT.Copy, scale=cr("kdec")[:, bass.ds(h, 1)]).then_inc(kd_done, 1)
                rows_copy(0)
                for g in range(2):
                    act.wait_ge(ks_high, 2 * h + g + 1)
                    src, dst = slice(32 * g, 32 * g + 32), slice(32 - 32 * g, 64 - 32 * g)
                    act.activation(KS[dst, 4 * g:4 * g + 4, :], KS[src, 4 * g:4 * g + 4, :].bitcast(F32), ACT.Copy) \
                        .then_inc(ks_copied, 1)
                for c in range(1, 5):
                    a = W0 + P * (c - 1)
                    act.wait_ge(o_ready, 5 * h + c)
                    act.activation(O[:, :, a:a + P], PS[:, 4 + c % 2, :].rearrange("p (v n) -> p v n", v=4), ACT.Copy) \
                        .then_inc(o_evac, 1)
                    if c in (2, 3):
                        states_out(2 * c - 4)
                        states_out(2 * c - 3)
                act.wait_ge(o_evac, 5 * h + 4)
                squares(1)
                rows_copy(1)
                act.wait_ge(o_ready, 5 * h + 5)
                act.activation(O[:, :, 0:W0], PS[:, 2, 0:4 * W0].rearrange("p (v n) -> p v n", v=4), ACT.Copy) \
                    .then_inc(o_evac, 1)
                act.wait_ge(o_evac, 5 * h + 5)
                act.wait_ge(osq_used, 2 * h + 1)
                squares(0)
                act.wait_ge(s_done, 5 * h + 5)
                act.dma_start(io["state_ret_prompt"][0, 0, bass.ds(h, 1)].rearrange("o (t p) e -> p (o t) e", p=P),
                              S[:]).then_inc(s_stored, 16)
                for b in range(4, DB):
                    states_out(b)
                act.wait_ge(osq_used, 2 * h + 2)
                inverse_root(PS[:, 4:6, 0:HF], DV, oroot_done, 2 * h)
                for s in range(4):
                    act.wait_ge(sb_stored[s], 32 * h + 32)
                for v in range(4):
                    if last_head and v % 2 == 0:
                        gate(n, h, [v // 2])
                    act.wait_ge(y_done, 4 * h + v + 1)
                    act.activation(YH[:, v, :], O[:, v, :], ACT.Copy).then_inc(yhi_done, 1)

            with act.Fori(0, RH - 1) as h:
                n = Blk(N_RET, 5 * h)
                retention(n, h)
                for j in range(8):
                    w_hi(n + 4 + j)
            n = Blk(N_RET + 10 * (RH - 1))
            retention(n, RH - 1, last_head=True)
            for j in range(3):
                w_hi(n + 4 + j)
                block_squares(1, n + 2 + j, j)
            block_squares(1, n + 5, 3)
            w_hi(n + 7)

            def mlp(n0, l):
                def up(n, k, j):
                    w_hi(n + 2)
                    act.wait_ge(evac_done, n.n + 3)
                    if j == 0:
                        act.wait_ge(unit_ready, n.n + 2)
                    act.activation(HH[:, 2 * j:2 * j + 2, :].rearrange("p m (a n) -> p m a n", a=2),
                                   HT[:], ACT.Square).then_inc(hhi_done, 1)
                with act.Fori(0, 3) as c:
                    n = Blk(n0, 4 * c)
                    for j in range(4):
                        up(n + j, 16 * l + 4 * c, j)
                    for j in range(4):
                        w_hi(n + 4 + j + 2)
                n = Blk(n0 + 24)
                for j in range(4):
                    up(n + j, 16 * l + 12, j)
                for j in range(4):
                    squares_too = l == 0
                    if squares_too and j == 3:
                        block_squares(2, n + 4 + j, j)
                    if n.c + 4 + j + 2 < N_END:
                        w_hi(n + 4 + j + 2)
                    if squares_too and j < 3:
                        block_squares(2, n + 4 + j, j)
            norm(1, N_MLP0)
            act.wait_ge(s_stored, 16 * RH + 16)
            mlp(N_MLP0, 0)

            norm(2, N_KVF)
            w_hi(Blk(N_KVF + 2))
            act.wait_ge(f_neg, 1)
            f = TT[0:FH, 1, :]
            act.activation(f, f, ACT.Exp).then_inc(f_exp, 1)
            act.wait_ge(f_exp, 1)
            act.activation(f, f, ACT.Ln, bias=1.0).then_inc(f_ln, 1)

            def by_head(k):
                sq = TT[:].rearrange("p a n -> p (a n)")[:, 0:D]
                for w in range(5):
                    if w == 0:
                        act.wait_ge(evac_done, (N_KVF + 5 if k == 0 else N_QG + 4) + 2)
                    if k or w:
                        act.wait_ge(sqt_used, 5 * k + w)
                    act.activation(sq, TOK[:, w, :], ACT.Square).then_inc(sqt_done, 1)
                act.wait_ge(sqt_used, 5 * k + 5)
                act.activation(SS[:], SS[:], ACT.Sqrt, scale=1.0 / DH, bias=ck("eps")).then_inc(hroot_done, 1)

            def turn(dst, first, scale):
                for t in range(KT):
                    act.wait_ge(tok_turned, first + t + 1)
                    act.activation(dst[:, t, 0:T - P], PS[:, 2 * (t % 4), 0:T - P], ACT.Copy, scale=scale)
                    act.activation(dst[:, t, T - P:T], PS[:, 2 * (t % 4) + 1, 0:P], ACT.Copy, scale=scale) \
                        .then_inc(tok_evac, 1)

            for j in range(4):
                w_hi(Blk(N_KVF + 3 + j))
            by_head(0)
            for j in range(4):
                w_hi(Blk(N_KVF + 7 + j))
            act.wait_ge(evac_done, N_QG + 2)
            out_v = [(io["v_prompt"][0, NMETA:].rearrange("(c p) h d -> p c (h d)", p=P), VV[:, 1:5, :]),
                     (io["v_prompt"][0, 0:NMETA].rearrange("p h d -> p (h d)"), VV[NSAMP:W0, 0, :]),
                     (io["v_sample"].rearrange("b s h d -> (b s) (h d)"), VV[0:NSAMP, 0, :])]
            out_k = [(io["k_prompt"][0, NMETA:].rearrange("(c p) h d -> p c (h d)", p=P), TOK[:, 1:5, :]),
                     (io["k_prompt"][0, 0:NMETA].rearrange("p h d -> p (h d)"), TOK[NSAMP:W0, 0, :]),
                     (io["k_sample"].rearrange("b s h d -> (b s) (h d)"), TOK[0:NSAMP, 0, :])]
            out_f = [(io["logf_prompt"][0, NMETA:].rearrange("(c p) h -> p c h", p=P), LFO[:, 1:5, :]),
                     (io["logf_prompt"][0, 0:NMETA], LFO[NSAMP:W0, 0, :]),
                     (io["logf_sample"].rearrange("b s h -> (b s) h"), LFO[0:NSAMP, 0, :])]
            for dst, src in out_v:
                act.dma_start(dst, src).then_inc(out_stored, 16)
            act.wait_ge(tok_done, 5)
            for dst, src in out_k:
                act.dma_start(dst, src).then_inc(k_stored, 16)
            act.wait_ge(small_done, 1)
            for dst, src in out_f:
                act.dma_start(dst, src).then_inc(out_stored, 16)
            turn(KTT, 0, 1.0)
            act.wait_ge(tok_evac, KT)
            norm(3, N_QG)
            for j in range(4):
                w_hi(Blk(N_QG + 2 + j))
            by_head(1)
            act.activation(NSR[:], NS[:, 0:FH * P], ACT.Copy).then_inc(rounded, 1)
            for j in range(4):
                n = Blk(N_QG + 4 + j)
                w_hi(n + 2)
                act.wait_ge(unit_ready, n.n + 3)
                act.activation(GG[:, 2 * j:2 * j + 2, :].rearrange("p m (a n) -> p m a n", a=2),
                               PS[:, 4 * n.slot:4 * n.slot + 4, 0:HF].rearrange("p (m a) n -> p m a n", a=2),
                               ACT.Sigmoid).then_inc(gate_done, 1)
            act.wait_ge(unit_ready, N_OUT + 2)
            turn(QT, KT, GK[:, 1:2])

            def exp(j):
                for par in range(2):
                    i = 2 * (j % 2) + par
                    act.wait_ge(mx_done, 2 * j + par + 1)
                    if j >= 2:
                        act.wait_ge(pt_ready, j - 1)
                    act.activation(PP[j % 2][par][:, 0:keys_of(j % 4)], score_cols(j, par), ACT.Exp,
                                   bias=NM[:, i:i + 1], accum_out=SM[:, i:i + 1]).then_inc(ex_done, 1)

            exp(0)
            for j in range(4 * KT):
                if j + 1 < 4 * KT and j % 4 != 2:
                    exp(j + 1)
                n = P * (j % 4 + 1)
                act.wait_ge(pt_ready, j + 1)
                meta = PS[0:NMETA, out_banks(j)[0], 0:2 * P].rearrange("p (a n) -> p a n", a=2)
                act.activation(PTM[NSAMP:W0], meta, ACT.Copy).then_inc(pt_evac, 1)
                act.activation(PTS[:, :, 0:n], PS[:, 6:8, 0:n], ACT.Copy).then_inc(pt_evac, 1)
                if j % 4 == 2:
                    exp(j + 1)

            def exp_s(b):
                act.wait_ge(smx_done, b + 1)
                act.activation(PB[:], PS[:, 0:3, :].rearrange("p a n -> p (a n)")[:, 0:SK], ACT.Exp, bias=NM[:, 2:3],
                               accum_out=SM[:, 2:3]).then_inc(sex_done, 1)

            def slot(b, what):
                s = turn_bank(b, what)
                return PS[:, s:s + 2, :].rearrange("p a (t n) -> p (a t) n", n=P)

            def page_copy(b, p):
                kn = NPAGE * b + p
                act.wait_ge(k_used, kn + 1)
                if kn:
                    act.wait_ge(kp_evac, turn_no(b, p))
                if kn >= 2:
                    act.wait_ge(sc_used, kn - 1)
                act.activation(KP[kn % 2][:], slot(b, p), ACT.Copy).then_inc(kp_evac, 1)

            def probs_copy(b):
                act.wait_ge(spt_ready, 2 * b + 1)
                act.wait_ge(kp_evac, turn_no(b + 1, "probs"))
                act.activation(PSM[:], slot(b + 1, "probs"), ACT.Copy).then_inc(kp_evac, 1)

            def new_probs_copy(b):
                act.wait_ge(spt_ready, 2 * b + 2)
                act.activation(PSN[:], PS[0:NSAMP, turn_bank(b + 1, "new"), 0:P], ACT.Copy).then_inc(kp_evac, 1)

            for b in range(DB + 1):
                if b == 0:
                    page_copy(b, 0)
                    page_copy(b, 1)
                else:
                    exp_s(b - 1)
                    probs_copy(b - 1)
                if b < DB:
                    page_copy(b, 2)
                    page_copy(b, 3)
                if b > 0:
                    new_probs_copy(b - 1)
                if b < DB:
                    for p in range(4, NPAGE):
                        page_copy(b, p)

            act.wait_ge(ot_done, 2 * DB)
            for t in range(KT):
                act.activation(XH[:, t, :], GG[:, t, :], ACT.Copy).then_inc(fyhi_done, 1)
            for j in range(3):
                w_hi(Blk(N_OUT + 2 + j))
                block_squares(4, Blk(N_OUT + j), j)
            block_squares(4, Blk(N_OUT + 3), 3)
            w_hi(Blk(N_OUT + 5))
            norm(4, N_MLP1)
            mlp(N_MLP1, 1)
            for k in range(10):
                n = WINDOWS[k // 2][1]
                act.wait_ge(yo_ready, k + 1)
                act.activation(YO[0:n, k // 2, 512 * (k % 2):512 * (k % 2) + 512], PS[0:n, k % 8, :], ACT.Copy) \
                    .then_inc(yo_done, 1)
            act.wait_ge(out_stored, 16 * 6)

        @block.vector
        def _(dve):
            dve.sem_inc(evac_done, 2)
            dve.sem_inc(s_stored, 16)
            step = Tally(dve_step)

            def do(ins):
                dve.wait_ge(dve_step, step.mark(ins))

            def add_squares(k, j):
                f = norm_full(k)
                for t in (2 * j, 2 * j + 1):
                    dve.wait_ge(sq_done, KT * f + t + 1)
                    if t == 1:
                        dve.tensor_tensor(RR[:], TT[:, 0, :], TT[:, 1, :], ALU.add).then_inc(sq_used, 2)
                    if t > 1:
                        dve.wait_ge(sq_used, KT * f + t)
                        dve.tensor_tensor(RR[:], RR[:], TT[:, t % 2, :], ALU.add).then_inc(sq_used, 1)

            def norm(k):
                f = norm_full(k)
                if f is not None:
                    dve.wait_ge(root_done, 2 * f + 2)

                def low(t):
                    dve.wait_ge(xhi_done, KT * k + t + 1)
                    dve.tensor_tensor(XL[:, t, :], TT[:, t % 2, :], XH[:, t, :].bitcast(F32), ALU.subtract) \
                        .then_inc(xlo_done, 1)

                for t in range(KT):
                    if t >= 2:
                        low(t - 2)
                        dve.wait_ge(xlo_done, KT * k + t - 1)
                    dve.scalar_tensor_tensor(TT[:, t % 2, :], X[:, t, :], GN[:, k, t:t + 1], RR[:], ALU.mult,
                                             ALU.mult).then_inc(xn_done, 1)
                low(KT - 2)
                low(KT - 1)
                dve.wait_ge(xlo_done, KT * (k + 1))

            def halves(x):
                return x.rearrange("p (a n) -> p a n", a=2)

            def begin(n):
                dve.wait_ge(unit_ready, n.n + 3)
                dve.wait_ge(evac_done, n.n + 2)

            def rotate(n, dst, last_on_rot):
                begin(n)
                x1, x2 = (PS[:, 4 * n.slot + 2 * m:4 * n.slot + 2 * m + 2, 0:HF] for m in range(2))
                cos, sin = halves(cr("cos")), halves(cr("sin"))
                t1, t2 = halves(TT[:, 0, :]), halves(TT[:, 1, :])
                step.mark(dve.tensor_tensor(t1, x1, cos, ALU.mult))
                do(dve.tensor_tensor(t2, x2, sin, ALU.mult))
                do(dve.tensor_tensor(dst[:, 0, :], TT[:, 0, :], TT[:, 1, :], ALU.subtract))
                step.mark(dve.tensor_tensor(t1, x2, cos, ALU.mult))
                dve.tensor_tensor(t2, x1, sin, ALU.mult).then_inc(evac_done, 1)
                dve.wait_ge(evac_done, n.n + 3)
                ins = dve.tensor_tensor(dst[:, 1, :], TT[:, 0, :], TT[:, 1, :], ALU.add)
                if last_on_rot:
                    ins.then_inc(rot_done, 1)
                else:
                    do(ins)

            def qkv(n, h):
                rotate(n, Q, False)
                for d in range(2):
                    q4 = Q[:, d, W0:T].rearrange("p (c n) -> p c n", c=4)
                    o4 = QD[:, d, W0:T].rearrange("p (c n) -> p c n", c=4)
                    g = cr("qdec")[:, bass.ds(P * h, P)].rearrange("p (o n) -> p o n", o=1).to_broadcast([P, 4, P])
                    dve.tensor_tensor(o4, q4, g, ALU.mult)
                g = cr("sqdec")[:, bass.ds(NSAMP * h, NSAMP)].rearrange("p (o n) -> p o n", o=1) \
                    .to_broadcast([P, 2, NSAMP])
                dve.tensor_tensor(QD[:, :, 0:NSAMP], Q[:, :, 0:NSAMP], g, ALU.mult).then_inc(rot_done, 1)
                rotate(n + 1, K, True)
                for j in range(2):
                    m = n + 2 + j
                    begin(m)
                    dve.tensor_copy(V[:, 0:4, BW * j:BW * j + BW].rearrange("p (a b) n -> p a b n", b=2),
                                    PS[:, 4 * m.slot:4 * m.slot + 2, :].rearrange("p a (b n) -> p a b n", b=2))
                    dve.tensor_copy(V[:, 4, BW * j:BW * j + BW], PS[:, 4 * m.slot + 2, 0:BW]).then_inc(evac_done, 1)

            def gate(n, h, js=range(2)):
                for j in js:
                    m = n + j
                    begin(m)
                    dve.wait_ge(sig_done, 2 * h + j + 1)
                    g = G[:, 2 * j:2 * j + 2, :].rearrange("p m (a n) -> p m a n", a=2)
                    src = PS[:, 4 * m.slot:4 * m.slot + 4, 0:HF].rearrange("p (m a) n -> p m a n", a=2)
                    dve.tensor_tensor(g, src, g, ALU.mult).then_inc(evac_done, 1)

            def retention(n, h, last_head=False):
                for g in range(2):
                    rows = slice(32 * g, 32 * g + 32)
                    dve.wait_ge(vs_high, 4 * h + 2 * g + 1)
                    dve.tensor_tensor(VS[32 - 32 * g:64 - 32 * g, g, :], V[rows, 0, :], VS[rows, g, :].bitcast(F32),
                                      ALU.subtract).then_inc(vs_done, 1)
                if not last_head:
                    gate(n, h)
                dve.wait_ge(at_ready, h + 1)
                g = cr("dec")[:, bass.ds(P * h, P)].rearrange("p (o n) -> p o n", o=1).to_broadcast([P, 4, P])
                dve.tensor_tensor(AT[:], PS[:, 0, :].rearrange("p (c n) -> p c n", c=4), g, ALU.mult)
                dve.tensor_tensor(AT0[:], PS[0:W0, 1, 0:W0], CR[0:W0, bass.ds(W0 * h + RET["dec0"][0], W0)],
                                  ALU.mult).then_inc(at_done, 1)
                dve.wait_ge(kt_ready, h + 1)
                at = RET["kdec0"][0]
                dve.tensor_scalar(KM[:], PS[0:W0, 4, 0:DK], CR[0:W0, bass.ds((DB + 1) * h + (at + DB), 1)], None,
                                  ALU.mult).then_inc(km_done, 1)
                for g in range(2):
                    rows = slice(32 * g, 32 * g + 32)
                    src = PS[rows, 4, 0:DK].rearrange("p (o n) -> p o n", o=1).to_broadcast([32, 4, DK])
                    d = CR[rows, bass.ds((DB + 1) * h + (at + 4 * g), 4)].rearrange("p (b o) -> p b o", o=1) \
                        .to_broadcast([32, 4, DK])
                    dve.tensor_tensor(KS[rows, 4 * g:4 * g + 4, :], src, d, ALU.mult).then_inc(ks_high, 1)
                up = PS[:, 6:8, :]
                dve.wait_ge(upd_ready, 5 * h + 1)
                dve.wait_ge(s_stored, 16 * h + 16)
                dve.tensor_copy(S[:], up).then_inc(s_done, 1)
                for b in range(DB):
                    rows = slice(32 * (b // 4), 32 * (b // 4) + 32)
                    if b % 4 == 0:
                        dve.wait_ge(ks_high, 2 * h + b // 4 + 1)
                    ins = dve.scalar_tensor_tensor(KS[64:96, b, :], PS[rows, 4, 0:DK],
                                                   CR[rows, bass.ds((DB + 1) * h + (at + b), 1)],
                                                   KS[rows, b, :].bitcast(F32), ALU.mult, ALU.subtract)
                    if b % 4 == 3:
                        ins.then_inc(ks_done, 1)
                def new_state(b, bk):
                    dve.wait_ge(supd_ready, 8 * h + b + 1)
                    dve.scalar_tensor_tensor(SB[b % 4][:], SB[b % 4][:], cr("g8")[:, bass.ds(h, 1)],
                                             PS[:, bk:bk + 2, :], ALU.mult, ALU.add).then_inc(sb_done, 1)

                for c in range(1, 5):
                    if c in (2, 3):
                        new_state(2 * c - 3, 0)
                    dve.wait_ge(upd_ready, 5 * h + c + 1)
                    dve.wait_ge(s_done, 5 * h + c)
                    dve.scalar_tensor_tensor(S[:], S[:], cr("gC")[:, bass.ds(h, 1)], up, ALU.mult, ALU.add) \
                        .then_inc(s_done, 1)
                    if c < 3:
                        new_state(2 * c - 2, 0)
                for b in range(4, DB):
                    new_state(b, 0 if b % 2 == 0 else 6)
                dve.wait_ge(oroot_done, 2 * h + 2)
                for v in range(4):
                    do(dve.tensor_tensor(O[:, v, :], O[:, v, :], RR[:], ALU.mult))

                def y(v):
                    dve.tensor_tensor(O[:, v, :], O[:, v, :], G[:, v, :], ALU.mult).then_inc(y_done, 1)

                def y_low(v):
                    dve.wait_ge(yhi_done, 4 * h + v + 1)
                    dve.tensor_tensor(YL[:, v, :], O[:, v, :], YH[:, v, :].bitcast(F32), ALU.subtract) \
                        .then_inc(ylo_done, 1)

                if last_head:
                    for j in range(2):
                        gate(n, h, [j])
                        dve.wait_ge(evac_done, (n + j).n + 3)
                        y(2 * j)
                        y(2 * j + 1)
                        y_low(2 * j)
                        y_low(2 * j + 1)
                else:
                    for v in range(4):
                        y(v)
                    for v in range(4):
                        y_low(v)
                dve.wait_ge(ylo_done, 4 * h + 4)

            def residual(n, j):
                begin(n)
                x = X[:, 2 * j:2 * j + 2, :].rearrange("p m (a n) -> p m a n", a=2)
                src = PS[:, 4 * n.slot:4 * n.slot + 4, 0:HF].rearrange("p (m a) n -> p m a n", a=2)
                dve.tensor_tensor(x, src, x, ALU.add).then_inc(evac_done, 1)

            for j in range(4):
                add_squares(0, j)
            norm(0)
            qkv(Blk(0), 0)
            PER_HEAD = 13
            with dve.Fori(0, RH - 1) as h:
                step.enter(h, PER_HEAD)
                n = Blk(N_RET, 5 * h)
                retention(n, h)
                qkv(n + 2, h + 1)
                for j in range(4):
                    residual(n + 6 + j, j)
            step.leave(PER_HEAD, RH - 1)
            n = Blk(N_RET + 10 * (RH - 1))
            retention(n, RH - 1, last_head=True)
            for j in range(4):
                residual(n + 2 + j, j)
                add_squares(1, j)

            def mlp(n0, l):
                def chunk(c):
                    n = Blk(n0, 4 * c)
                    k = 16 * l + 4 * c
                    for j in range(4):
                        m = n + j
                        begin(m)
                        if j:
                            dve.wait_ge(hhi_done, k + j)
                            dve.wait_ge(hlo_done, k + j)
                        src = PS[:, 4 * m.slot:4 * m.slot + 4, 0:HF].rearrange("p (m a) n -> p m a n", a=2)
                        dve.tensor_scalar(HT[:], src, 0.0, None, ALU.max).then_inc(evac_done, 1)
                        lo = HL[:, 2 * j:2 * j + 2, :].rearrange("p m (a n) -> p m a n", a=2)
                        hi = HH[:, 2 * j:2 * j + 2, :].bitcast(F32).rearrange("p m (a n) -> p m a n", a=2)
                        dve.wait_ge(hhi_done, k + j + 1)
                        dve.tensor_tensor(HT[:], HT[:], HT[:], ALU.mult).then_inc(sqh_done, 1)
                        dve.wait_ge(sqh_done, k + j + 1)
                        dve.tensor_tensor(lo, HT[:], hi, ALU.subtract).then_inc(hlo_done, 1)
                    for j in range(4):
                        residual(n + 4 + j, j)
                        if l == 0 and isinstance(c, int):
                            add_squares(2, j)
                with dve.Fori(0, 3) as c:
                    chunk(c)
                chunk(3)
            norm(1)
            dve.wait_ge(s_stored, 16 * RH + 16)
            mlp(N_MLP0, 0)

            norm(2)
            n = Blk(N_KVF)
            begin(n)
            f0, f1 = TT[0:FH, 0, :], TT[0:FH, 1, :]
            dve.tensor_scalar(halves(f0), PS[0:FH, 4 * n.slot:4 * n.slot + 2, 0:HF], BF[:], None, ALU.add) \
                .then_inc(evac_done, 1)
            dve.wait_ge(evac_done, n.n + 3)
            dve.scalar_tensor_tensor(f1, f0, -1.0, f0, ALU.mult, ALU.min).then_inc(f_neg, 1)
            dve.wait_ge(f_ln, 1)
            dve.scalar_tensor_tensor(LF[:], f0, 0.0, f1, ALU.min, ALU.subtract).then_inc(lf_done, 1)
            dve.wait_ge(lf_done, 1)
            ones = ck("one")
            cum = TT[0:FH, 0, 0:NKEY]
            do(dve.tensor_tensor_scan(cum, ones[0:FH].to_broadcast([FH, NKEY]), LF[:, NSAMP:T], 0.0, ALU.mult, ALU.add))
            do(dve.memset(CU[:].bitcast(F32), 0.0))
            do(dve.tensor_copy(CU[0:FH, :], cum))
            do(dve.tensor_tensor(CU[32:32 + FH, :], cum, CU[0:FH, :].bitcast(F32), ALU.subtract))
            dve.sem_inc(lf_done, 1)

            def evac_tok(n, dst, j):
                begin(n)
                c = slice(BW * j, BW * j + BW)
                dve.tensor_copy(dst[:, 0:4, c].rearrange("p (a b) n -> p a b n", b=2),
                                PS[:, 4 * n.slot:4 * n.slot + 2, :].rearrange("p a (b n) -> p a b n", b=2))
                dve.tensor_copy(dst[:, 4, c], PS[:, 4 * n.slot + 2, 0:BW]).then_inc(evac_done, 1)

            def by_head(k, gain):
                sq = TT[:].rearrange("p a n -> p (a n)")[:, 0:D].rearrange("p (h d) -> p h d", d=DH)
                for w in range(5):
                    dve.wait_ge(sqt_done, 5 * k + w + 1)
                    dve.reduce_sum(SS[:, w, :], sq, AX).then_inc(sqt_used, 1)
                dve.wait_ge(hroot_done, k + 1)
                do(dve.reciprocal(SS[:], SS[:]))
                for w in range(5):
                    x = TOK[:, w, :].rearrange("p (h d) -> p h d", d=DH)
                    r = SS[:, w, :].rearrange("p (h o) -> p h o", o=1).to_broadcast([P, FH, DH])
                    ins = dve.tensor_tensor(x, x, r, ALU.mult)
                    if gain is not None:
                        do(ins)
                        g = gain.rearrange("p (o d) -> p o d", o=1).to_broadcast([P, FH, DH])
                        ins = dve.tensor_tensor(x, x, g, ALU.mult)
                    ins.then_inc(tok_done, 1)

            for j in range(4):
                evac_tok(Blk(N_KVF + 1 + j), TOK, j)
            dve.wait_ge(fox_in, 16 * 5)
            by_head(0, GKB[:])
            do(dve.tensor_scalar(GK[:, 1:2], GK[:, 1:2], DH ** -0.5, None, ALU.mult))
            for j in range(4):
                evac_tok(Blk(N_KVF + 5 + j), VV, j)
            dve.wait_ge(small_ready, 1)
            dve.tensor_copy(LFO[0:W0, 0, :], PS[0:W0, 0, 0:FH])
            dve.tensor_copy(LFO[:, 1:5, :], PS[:, 0, FH:5 * FH].rearrange("p (w h) -> p w h", h=FH))
            dve.tensor_tensor(LS[:], PS[:, 1, 0:NSAMP], cf("own"), ALU.mult).then_inc(small_done, 1)
            norm(3)
            dve.wait_ge(k_stored, 48)
            dve.wait_ge(tok_evac, KT)
            for j in range(4):
                evac_tok(Blk(N_QG + j), TOK, j)
            by_head(1, None)
            for j in range(4):
                dve.wait_ge(gate_done, j + 1)
                dve.sem_inc(evac_done, 1)
            dve.wait_ge(lfk_ready, 1)
            for i in range(2):
                dve.tensor_copy(LFK[:].rearrange("k p b h -> k h b p")[:, 8 * i:8 * i + 8],
                                PS[:, i, :].rearrange("k (h b p) -> k h b p", h=8, b=DB)).then_inc(lfk_done, 1)
            dve.wait_ge(lfc_ready, 1)
            dve.tensor_tensor_scan(CL[:, 0:PAST], ones.to_broadcast([P, PAST]),
                                   PS[:, 2:4, :].rearrange("p a n -> p (a n)"), 0.0, ALU.mult, ALU.add) \
                .then_inc(lfc_done, 1)
            dve.wait_ge(lfc_done, 1)
            dve.tensor_tensor_scan(CL[:, PAST:SK], ones.to_broadcast([P, NSAMP]), LS[:], CL[:, PAST - 1:PAST],
                                   ALU.mult, ALU.add).then_inc(lfc_done, 1)

            def maximum(j, par):
                n = keys_of(j % 4)
                i = 2 * (j % 2) + par
                dve.wait_ge(s_ready, 2 * j + par + 1)
                own = score_cols(j, par)[:, n - P:n]
                dve.tensor_tensor(own, own, cf("causal"), ALU.add).then_inc(masked, 1)
                dve.wait_ge(masked, 2 * j + par + 1)
                dve.tensor_reduce(NM[:, i:i + 1], score_cols(j, par), AX, ALU.max, negate=True).then_inc(mx_done, 1)

            def normed_probs(j):
                n = keys_of(j % 4)
                for par in range(2):
                    i = 2 * (j % 2) + par
                    dve.wait_ge(ex_done, 2 * j + par + 1)
                    dve.reciprocal(RM[:, i:i + 1], SM[:, i:i + 1]).then_inc(inv_row, 1)
                for par in range(2):
                    i = 2 * (j % 2) + par
                    dve.wait_ge(inv_row, 2 * j + par + 1)
                    dve.tensor_scalar(PP[j % 2][par][:, 0:n], PP[j % 2][par][:, 0:n], RM[:, i:i + 1], None, ALU.mult) \
                        .then_inc(pn_done, 1)

            def gated(j):
                t, qb = j // 4, j % 4
                dve.wait_ge(pv_ready, j + 1)
                g = GG[:, t, W0 + P * qb:W0 + P * qb + P]
                dve.tensor_tensor(g, PS[:, out_banks(j)[1], 256:384], g, ALU.mult).then_inc(pv_evac, 1)

            def by_pair(t):
                for par in range(2):
                    h = slice(DH * par, DH * par + DH)
                    ins = dve.tensor_copy(QZ[t % 2][h, par, :], QT[h, t, W0:T])
                ins.then_inc(qz_done, 1)

            dve.wait_ge(qz_zero, 2)
            dve.wait_ge(tok_evac, 2 * KT)
            by_pair(0)
            maximum(0, 0)
            maximum(0, 1)
            normed_probs(0)
            maximum(1, 0)
            maximum(1, 1)
            for j in range(4 * KT):
                if j % 4 == 0 and j + 4 < 4 * KT:
                    by_pair(j // 4 + 1)
                late = j % 4 == 2
                if j + 1 < 4 * KT and not late:
                    normed_probs(j + 1)
                if j + 2 < 4 * KT:
                    maximum(j + 2, 0)
                if not scores_first(j):
                    gated(j)
                if late:
                    normed_probs(j + 1)
                if j + 2 < 4 * KT:
                    maximum(j + 2, 1)
                if scores_first(j):
                    gated(j)

            do(dve.memset(QB[:], 0.0))

            def queries(b):
                if b >= 2:
                    dve.wait_ge(ss_ready, b - 1)
                for par in range(2):
                    r = slice(DH * par, DH * par + DH)
                    for e in range(2):
                        a = 48 * e + DS * par
                        q = QT[r].rearrange("p (g e) n -> p g e n", e=2)[:, :, e, DS * b:DS * b + DS]
                        ins = dve.tensor_copy(QB[r, b % 2, :, a:a + DS], q)
                ins.then_inc(qb_done, 1)

            def maxima_s(b):
                dve.wait_ge(ss_ready, b + 1)
                m = cf("newmask")[:, NSAMP * b:NSAMP * b + NSAMP]
                do(dve.tensor_tensor(PS[:, 2, 0:NSAMP], PS[:, 2, 0:NSAMP], m, ALU.add))
                dve.tensor_reduce(NM[:, 2:3], PS[:, 0:3, :].rearrange("p a n -> p (a n)")[:, 0:SK], AX, ALU.max,
                                  negate=True).then_inc(smx_done, 1)

            def output_s(b):
                dve.wait_ge(spv_ready, b + 1)
                dve.wait_ge(sex_done, b + 1)
                pick = cf("headpick").rearrange("p (h o) -> p h o", o=1).to_broadcast([P, 4, DH])
                do(dve.reciprocal(RM[:, 2:3], SM[:, 2:3]))
                do(dve.tensor_tensor(OX[:], PS[:, 3, 0:256].rearrange("p (h d) -> p h d", d=DH), pick, ALU.mult))
                do(dve.reduce_sum(OS[:], OX[:].rearrange("p h d -> p d h"), AX))
                dve.tensor_scalar(OS[:], OS[:], RM[:, 2:3], None, ALU.mult).then_inc(os_done, 1)

            def gated_s(b):
                dve.wait_ge(ot_ready, b + 1)
                for par in range(2):
                    r = slice(DH * par, DH * par + DH)
                    g = GG[r, :, DS * b:DS * b + DS]
                    o = PS[0:DH, 3, 256:384].rearrange("p (t c q) -> p t c q", c=2, q=DS)[:, :, par, :]
                    dve.tensor_tensor(g, o, g, ALU.mult).then_inc(ot_done, 1)

            def page_copy(b, p):
                kn = NPAGE * b + p
                dve.wait_ge(k_used, kn + 1)
                dve.wait_ge(kp_evac, turn_no(b, p))
                dve.wait_ge(sc_used, kn - 1)
                s = turn_bank(b, p)
                dve.tensor_copy(KP[kn % 2][:], PS[:, s:s + 2, :].rearrange("p a (t n) -> p (a t) n", n=P)) \
                    .then_inc(kp_evac, 1)

            queries(0)
            for b in range(DB):
                if b + 1 < DB:
                    queries(b + 1)
                if b:
                    output_s(b - 1)
                maxima_s(b)
                if b:
                    gated_s(b - 1)
                if b + 1 < DB:
                    page_copy(b + 1, 0)
                    page_copy(b + 1, 1)
            output_s(DB - 1)
            gated_s(DB - 1)

            for t in range(KT):
                dve.wait_ge(fyhi_done, t + 1)
                dve.tensor_tensor(XL[:, t, :], GG[:, t, :], XH[:, t, :].bitcast(F32), ALU.subtract) \
                    .then_inc(fylo_done, 1)
            for j in range(4):
                residual(Blk(N_OUT + j), j)
                add_squares(4, j)
            norm(4)
            mlp(N_MLP1, 1)


_INS = ["x_prompt", "x_sample", "state_ret", "cache_k", "cache_v", "cache_logf", "page_table", "meta", "g_attn", "g_mlp",
        "w_ret_in", "w_ret_out", "g_kv", "w_kvf", "b_f", "g_k", "w_fox_qg", "g_q", "w_fox_out", "w_mlp_up",
        "w_mlp_down"]
_OUTS = [("y_prompt", (1, NPROMPT, D)), ("y_sample", (DB, DS, D)), ("state_ret_prompt", (1, 1, RH, DK, DV)),
         ("state_ret_sample", (1, DB, RH, DK, DV)), ("k_prompt", (1, NKEY, FH, DH)), ("v_prompt", (1, NKEY, FH, DH)),
         ("logf_prompt", (1, NKEY, FH)), ("k_sample", (DB, DS, FH, DH)), ("v_sample", (DB, DS, FH, DH)),
         ("logf_sample", (DB, DS, FH))]


def build(nc, arrays):
    io = {}
    for name, a in arrays.items():
        io[name] = nc.dram_tensor(f"in_{name}", a.shape, mybir.dt.from_np(a.dtype), kind="ExternalInput").ap()
    for name, shape in _OUTS:
        io[name] = nc.dram_tensor(f"out_{name}", shape, F32, kind="ExternalOutput").ap()
    program(nc, io)


def kernel(**inputs):
    import concourse.bacc as bacc
    from concourse.bass_utils import run_bass_kernel_spmd

    arrays = {name: np.ascontiguousarray(inputs[name]) for name in _INS}
    arrays.update(constants())
    nc = bacc.Bacc("TRN2", target_bir_lowering=False, num_devices=1)
    build(nc, arrays)
    r = run_bass_kernel_spmd(nc, [{f"in_{k}": v for k, v in arrays.items()}], core_ids=[0])
    return tuple(r.results[0][f"out_{name}"] for name, _ in _OUTS)
```
